# Optimizing a Trainium2 kernel written in Bass

```python
import jax, jax.numpy as jnp
from jax import lax
import numpy as np

D_MODEL = 1024
BATCH = 1
SEQ = 256
DEPTH = 2
DEC_BATCH = 8
DEC_SEQ = 4
PAST_LEN = 1024
PAGE_SIZE = 128

N_MIXERS = 2
N_CHUNK_LAYERS = (DEPTH + 1) // 2
N_ATTN_LAYERS = DEPTH // 2
CHUNK = 128
CHUNK_WIDTH = D_MODEL
CHUNK_GROUPS = 4
CHUNK_GROUP_DIM = CHUNK_WIDTH // CHUNK_GROUPS
HEAD_DIM = 128
N_HEADS = D_MODEL // HEAD_DIM
N_KV_HEADS = N_HEADS // 2
KV_GROUP = N_HEADS // N_KV_HEADS
ROT_DIM = HEAD_DIM // 4
ROPE_THETA = 500000.0
MOBA_BLOCK = 256
MOBA_TOP_K = 3
Q_BLOCK = 8
N_EXPERT_GROUPS = 4
EXPERTS_PER_GROUP = 4
N_EXPERTS = N_EXPERT_GROUPS * EXPERTS_PER_GROUP
TOP_K_IN_GROUP = 2
D_EXPERT = D_MODEL // 4
NORM_EPS = 1e-6
NEG_INF = -1e30

kernel_name = 'hybrid_chunkmlp_moba_hmoe_step'

def rms_norm(x, g):
    xf = x.astype(jnp.float32)
    y = xf * lax.rsqrt(jnp.mean(xf * xf, axis=-1, keepdims=True) + NORM_EPS)
    return (y * g.astype(jnp.float32)).astype(x.dtype)

def rope(x, pos):
    half = ROT_DIM // 2
    inv_freq = jnp.power(ROPE_THETA, -jnp.arange(half, dtype=jnp.float32) * 2.0 / ROT_DIM)
    ang = pos.astype(jnp.float32)[:, None] * inv_freq[None, :]
    cos = jnp.cos(ang)[None, :, None, :]
    sin = jnp.sin(ang)[None, :, None, :]
    xr = x[..., :ROT_DIM].astype(jnp.float32)
    x1, x2 = xr[..., :half], xr[..., half:]
    rot = jnp.concatenate([x1 * cos - x2 * sin, x2 * cos + x1 * sin], axis=-1).astype(x.dtype)
    return jnp.concatenate([rot, x[..., ROT_DIM:]], axis=-1)

def chunk_spatial_gating(h, w_in, g_v, w_s, b_s, w_out):
    B, L, _ = h.shape
    z = jax.nn.gelu(h @ w_in)
    u, v = z[..., :CHUNK_WIDTH], z[..., CHUNK_WIDTH:]
    v = rms_norm(v, g_v)
    n_chunks = -(-L // CHUNK)
    pad = n_chunks * CHUNK - L
    vc = jnp.pad(v, ((0, 0), (0, pad), (0, 0))).reshape(B, n_chunks, CHUNK, CHUNK_GROUPS, CHUNK_GROUP_DIM)
    causal = jnp.tril(jnp.ones((CHUNK, CHUNK), w_s.dtype))
    s = jnp.einsum('gts,bcsgd->bctgd', w_s * causal, vc) + jnp.transpose(b_s)[None, None, :, :, None]
    s = s.reshape(B, n_chunks * CHUNK, CHUNK_WIDTH)[:, :L]
    return (u * s) @ w_out, v

def attn_qkv(h, pos, w_qkv, q_norm, k_norm):
    B, T, _ = h.shape
    qkv = h @ w_qkv
    nq = N_HEADS * HEAD_DIM
    nk = N_KV_HEADS * HEAD_DIM
    q = qkv[..., :nq].reshape(B, T, N_HEADS, HEAD_DIM)
    k = qkv[..., nq:nq + nk].reshape(B, T, N_KV_HEADS, HEAD_DIM)
    v = qkv[..., nq + nk:].reshape(B, T, N_KV_HEADS, HEAD_DIM)
    q = rope(rms_norm(q, q_norm), pos)
    k = rope(rms_norm(k, k_norm), pos)
    return q, k, v

def moba_attention(q, k, v, q_pos):
    B, T = q.shape[0], q.shape[1]
    L = k.shape[1]
    nb = -(-L // MOBA_BLOCK)
    pad = nb * MOBA_BLOCK - L
    kb = jnp.pad(k, ((0, 0), (0, pad), (0, 0), (0, 0))).reshape(B, nb, MOBA_BLOCK, N_KV_HEADS, HEAD_DIM)
    vb = jnp.pad(v, ((0, 0), (0, pad), (0, 0), (0, 0))).reshape(B, nb, MOBA_BLOCK, N_KV_HEADS, HEAD_DIM)
    k_mean = jnp.mean(kb.astype(jnp.float32), axis=2)
    n_sel = min(MOBA_TOP_K, nb)
    qb = min(Q_BLOCK, T)
    n_qb = -(-T // qb)
    padq = n_qb * qb - T
    q_blocks = jnp.pad(q, ((0, 0), (0, padq), (0, 0), (0, 0))).reshape(B, n_qb, qb, N_HEADS, HEAD_DIM).transpose(1, 0, 2, 3, 4)
    pos_blocks = jnp.pad(q_pos, (0, padq), mode='edge').reshape(n_qb, qb)
    b_idx = jnp.arange(B)[:, None, None, None]
    h_idx = (jnp.arange(N_HEADS) // KV_GROUP)[None, None, :, None]
    blk_ids = jnp.arange(nb)
    sel_rank = jnp.arange(n_sel)
    in_blk = jnp.arange(MOBA_BLOCK)
    scale = HEAD_DIM ** -0.5

    def attend_block(args):
        qc, pc = args
        own = pc // MOBA_BLOCK
        qg = qc.astype(jnp.float32).reshape(B, qb, N_KV_HEADS, KV_GROUP, HEAD_DIM)
        gate = jnp.einsum('bqkgd,bnkd->bqkgn', qg, k_mean).reshape(B, qb, N_HEADS, nb)
        fully_past = blk_ids[None, :] < own[:, None]
        gate = jnp.where(fully_past[None, :, None, :], gate, NEG_INF)
        _, sel = lax.top_k(gate, n_sel)
        own_b = jnp.broadcast_to(own[None, :, None, None], (B, qb, N_HEADS, 1)).astype(sel.dtype)
        idx = jnp.concatenate([sel, own_b], axis=-1)
        gk = kb[b_idx, idx, :, h_idx]
        gv = vb[b_idx, idx, :, h_idx]
        blk_ok = jnp.concatenate([sel_rank[None, :] < own[:, None], jnp.ones((qb, 1), bool)], axis=-1)
        key_pos = idx[..., None] * MOBA_BLOCK + in_blk
        mask = blk_ok[None, :, None, :, None] & (key_pos <= pc[None, :, None, None, None])
        s = jnp.einsum('bqhd,bqhjkd->bqhjk', qc * scale, gk).astype(jnp.float32)
        s = jnp.where(mask, s, NEG_INF)
        p = jax.nn.softmax(s.reshape(B, qb, N_HEADS, -1), axis=-1).reshape(s.shape)
        return jnp.einsum('bqhjk,bqhjkd->bqhd', p.astype(gv.dtype), gv)

    out = lax.map(attend_block, (q_blocks, pos_blocks))
    return out.transpose(1, 0, 2, 3, 4).reshape(B, n_qb * qb, N_HEADS, HEAD_DIM)[:, :T]

def hier_moe(h, w_group, b_group, w_router, b_router, w_gate, w_up, w_down):
    B, T, D = h.shape
    x = h.reshape(B * T, D)
    g_prob = jax.nn.softmax((x @ w_group).astype(jnp.float32) + b_group.astype(jnp.float32), axis=-1)
    g_w, g_idx = lax.top_k(g_prob, 1)
    e_logits = ((x @ w_router).astype(jnp.float32) + b_router.astype(jnp.float32)).reshape(-1, N_EXPERT_GROUPS, EXPERTS_PER_GROUP)
    take = jnp.broadcast_to(g_idx[:, :, None], (g_idx.shape[0], 1, EXPERTS_PER_GROUP))
    e_logits = jnp.take_along_axis(e_logits, take, axis=1)[:, 0]
    e_prob = jax.nn.softmax(e_logits, axis=-1)
    e_w, e_idx = lax.top_k(e_prob, TOP_K_IN_GROUP)
    e_w = e_w / jnp.sum(e_w, axis=-1, keepdims=True) * g_w
    expert = g_idx * EXPERTS_PER_GROUP + e_idx
    gates = jnp.sum(jax.nn.one_hot(expert, N_EXPERTS, dtype=jnp.float32) * e_w[..., None], axis=1)
    a = jnp.einsum('nd,edf->nef', x, w_gate)
    b = jnp.einsum('nd,edf->nef', x, w_up)
    hid = jax.nn.silu(a) * b * gates[:, :, None].astype(x.dtype)
    y = jnp.einsum('nef,efd->nd', hid, w_down)
    return y.reshape(B, T, D)

def setup_inputs(seed: int = 0) -> dict:
    key = jax.random.key(seed)
    ks = jax.random.split(key, 24)
    f32 = jnp.float32
    n_pages = PAST_LEN // PAGE_SIZE
    n_pool = (DEC_BATCH * n_pages * 5) // 4
    qkv_cols = (N_HEADS + 2 * N_KV_HEADS) * HEAD_DIM

    def nrm(k, shape, scale=1.0):
        return jax.random.normal(k, shape, f32) * scale

    def gain(k, shape):
        return 1.0 + 0.02 * jax.random.normal(k, shape, f32)

    page_table = jax.random.permutation(ks[4], n_pool)[: DEC_BATCH * n_pages].reshape(DEC_BATCH, n_pages).astype(jnp.int32)
    return {
        'x_prompt': nrm(ks[0], (BATCH, SEQ, D_MODEL)),
        'x_sample': nrm(ks[1], (DEC_BATCH, DEC_SEQ, D_MODEL)),
        'cache_k': nrm(ks[2], (N_ATTN_LAYERS, n_pool, PAGE_SIZE, N_KV_HEADS, HEAD_DIM)),
        'cache_v': nrm(ks[3], (N_ATTN_LAYERS, n_pool, PAGE_SIZE, N_KV_HEADS, HEAD_DIM)),
        'page_table': page_table,
        'norm1': gain(ks[5], (DEPTH, D_MODEL)),
        'norm2': gain(ks[6], (DEPTH, D_MODEL)),
        'a_w_in': nrm(ks[7], (N_CHUNK_LAYERS, D_MODEL, 2 * CHUNK_WIDTH), D_MODEL ** -0.5),
        'a_g_v': gain(ks[8], (N_CHUNK_LAYERS, CHUNK_WIDTH)),
        'a_w_s': nrm(ks[9], (N_CHUNK_LAYERS, CHUNK_GROUPS, CHUNK, CHUNK), CHUNK ** -0.5),
        'a_b_s': 1.0 + 0.1 * jax.random.normal(ks[10], (N_CHUNK_LAYERS, CHUNK_GROUPS, CHUNK), f32),
        'a_w_out': nrm(ks[11], (N_CHUNK_LAYERS, CHUNK_WIDTH, D_MODEL), CHUNK_WIDTH ** -0.5),
        'b_w_qkv': nrm(ks[12], (N_ATTN_LAYERS, D_MODEL, qkv_cols), D_MODEL ** -0.5),
        'b_q_norm': gain(ks[13], (N_ATTN_LAYERS, HEAD_DIM)),
        'b_k_norm': gain(ks[14], (N_ATTN_LAYERS, HEAD_DIM)),
        'b_w_o': nrm(ks[15], (N_ATTN_LAYERS, N_HEADS * HEAD_DIM, D_MODEL), (N_HEADS * HEAD_DIM) ** -0.5),
        'moe_w_group': nrm(ks[16], (DEPTH, D_MODEL, N_EXPERT_GROUPS), D_MODEL ** -0.5),
        'moe_b_group': nrm(ks[17], (DEPTH, N_EXPERT_GROUPS), 0.01),
        'moe_w_router': nrm(ks[18], (DEPTH, D_MODEL, N_EXPERTS), D_MODEL ** -0.5),
        'moe_b_router': nrm(ks[19], (DEPTH, N_EXPERTS), 0.01),
        'moe_w_gate': nrm(ks[20], (DEPTH, N_EXPERTS, D_MODEL, D_EXPERT), D_MODEL ** -0.5),
        'moe_w_up': nrm(ks[21], (DEPTH, N_EXPERTS, D_MODEL, D_EXPERT), D_MODEL ** -0.5),
        'moe_w_down': nrm(ks[22], (DEPTH, N_EXPERTS, D_EXPERT, D_MODEL), D_EXPERT ** -0.5),
    }

def reference(x_prompt, x_sample, cache_k, cache_v, page_table, norm1, norm2,
              a_w_in, a_g_v, a_w_s, a_b_s, a_w_out,
              b_w_qkv, b_q_norm, b_k_norm, b_w_o,
              moe_w_group, moe_b_group, moe_w_router, moe_b_router,
              moe_w_gate, moe_w_up, moe_w_down):
    hp, hs = x_prompt, x_sample
    bp, tp = hp.shape[0], hp.shape[1]
    bs, ts = hs.shape[0], hs.shape[1]
    past_len = page_table.shape[1] * cache_k.shape[2]
    pos_p = jnp.arange(tp, dtype=jnp.int32)
    pos_s = past_len + jnp.arange(ts, dtype=jnp.int32)
    new_k_p, new_v_p, new_k_s, new_v_s, new_chunk_v = [], [], [], [], []
    for i in range(DEPTH):
        j = i // N_MIXERS
        np_in = rms_norm(hp, norm1[i])
        ns_in = rms_norm(hs, norm1[i])
        if i % N_MIXERS == 0:
            mp, _ = chunk_spatial_gating(np_in, a_w_in[j], a_g_v[j], a_w_s[j], a_b_s[j], a_w_out[j])
            ms, v_rows = chunk_spatial_gating(ns_in, a_w_in[j], a_g_v[j], a_w_s[j], a_b_s[j], a_w_out[j])
            new_chunk_v.append(v_rows)
        else:
            qp, kp, vp = attn_qkv(np_in, pos_p, b_w_qkv[j], b_q_norm[j], b_k_norm[j])
            op = moba_attention(qp, kp, vp, pos_p)
            qs, ks_new, vs_new = attn_qkv(ns_in, pos_s, b_w_qkv[j], b_q_norm[j], b_k_norm[j])
            past_k = cache_k[j][page_table].reshape(bs, past_len, N_KV_HEADS, HEAD_DIM)
            past_v = cache_v[j][page_table].reshape(bs, past_len, N_KV_HEADS, HEAD_DIM)
            k_all = jnp.concatenate([past_k, ks_new], axis=1)
            v_all = jnp.concatenate([past_v, vs_new], axis=1)
            os_ = moba_attention(qs, k_all, v_all, pos_s)
            mp = op.reshape(bp, tp, N_HEADS * HEAD_DIM) @ b_w_o[j]
            ms = os_.reshape(bs, ts, N_HEADS * HEAD_DIM) @ b_w_o[j]
            new_k_p.append(kp)
            new_v_p.append(vp)
            new_k_s.append(ks_new)
            new_v_s.append(vs_new)
        hp = hp + mp
        hs = hs + ms
        hp = hp + hier_moe(rms_norm(hp, norm2[i]), moe_w_group[i], moe_b_group[i], moe_w_router[i], moe_b_router[i], moe_w_gate[i], moe_w_up[i], moe_w_down[i])
        hs = hs + hier_moe(rms_norm(hs, norm2[i]), moe_w_group[i], moe_b_group[i], moe_w_router[i], moe_b_router[i], moe_w_gate[i], moe_w_up[i], moe_w_down[i])
    return (hp, hs, jnp.stack(new_k_p), jnp.stack(new_v_p), jnp.stack(new_k_s), jnp.stack(new_v_s), jnp.stack(new_chunk_v))


_drawn_inputs = setup_inputs


def setup_inputs(seed=0):
    import zlib

    import numpy as np

    out = dict(_drawn_inputs(seed))
    spreads = {}
    factors = {'a_g_v': 3.02,
     'b_q_norm': 8.0,
     'b_k_norm': 2.853,
     'moe_b_group': 4.633,
     'moe_b_router': 2.895}
    for name, (base, spread) in spreads.items():
        noise = np.random.default_rng([zlib.crc32(name.encode()), seed]).standard_normal(out[name].shape)
        drawn = base * np.exp(spread * noise) if base else spread * noise
        out[name] = __import__('jax').numpy.asarray(drawn.astype(out[name].dtype))
    for name, factor in factors.items():
        out[name] = (out[name] * factor).astype(out[name].dtype)
    return out
```

```python
from contextlib import ExitStack

import concourse.bass as bass
from concourse import mybir

F32 = mybir.dt.float32
I32 = mybir.dt.int32
ALU = mybir.AluOpType
ACT = mybir.ActivationFunctionType
AX = mybir.AxisListType

P = 128
EPS = 1e-6
NEG = -1e30
KV = 4
G = 2
NH = KV * G
ROT = 32
THETA = 500000.0
TOP_BLOCKS = 3
MOBA_BLOCK = 256
GRP = 4


def const_columns(T, TSA, TS):
    at, out = 0, {}
    for name, n in (("ident", P), ("keep_upper", P), ("causal_neg", P), ("cos", T), ("sin", T),
                    ("rotate", ROT), ("own_causal", TSA), ("own_neg", TSA * TSA // (GRP * TS)),
                    ("earlier", 16), ("later", 16), ("spread", TSA)):
        out[name] = slice(at, at + n)
        at += n
    return out, at


class Chain:

    def __init__(self, eng, sem, base=0):
        self.eng, self.sem, self.base, self.n = eng, sem, base, 0

    def link(self, ins):
        self.n += 1
        ins.then_inc(self.sem, 1)
        self.eng.wait_ge(self.sem, self.base + self.n)


def hybrid_step(nc, t, o):
    D = t["x_prompt"].shape[2]
    TP = t["x_prompt"].shape[1]
    NB, TS = t["x_sample"].shape[0:2]
    TSA = NB * TS
    T = TP + TSA
    DEPTH = t["norm1"].shape[0]
    KT = D // P
    CH = TP // P
    NT = CH + 1
    NPAGE = t["page_table"].shape[1]
    NPOOL = t["cache_k"].shape[1]
    ROWK = KV * P
    NE = t["moe_w_gate"].shape[1]
    EF = t["moe_w_gate"].shape[3]
    FB = EF // P
    SCALE = float(P) ** -0.5
    NG = NB // GRP
    QC = NH * TS
    BLK = NPAGE * P // MOBA_BLOCK
    EP = 4
    R5 = EP + NE
    NR = NT * R5 // EP
    LH = NH + KV
    TG = GRP * TS
    assert t["cache_k"].shape[2] == P and QC * GRP == P and DEPTH == 2 and NE == EP * EP and BLK == EP
    tok = [(c * P, P) for c in range(CH)] + [(TP, TSA)]
    cols, NCONST = const_columns(T, TSA, TS)

    with ExitStack() as ctx:
        def sb(name, shape, dt=F32):
            return ctx.enter_context(nc.sbuf_tensor(name, shape, dt))

        def sem(name):
            return ctx.enter_context(nc.semaphore(name))

        PS = ctx.enter_context(nc.psum_tensor("PS", [P, 8, 512], F32))

        half_a = sb("half_a", [P, KT * D])
        half_b = sb("half_b", [P, KT * D])
        w_a = half_a[:, :].rearrange("p (k n) -> p k n", k=KT)
        w_b = half_b[:, :].rearrange("p (k n) -> p k n", k=KT)
        k_pages = half_a[:, :].rearrange("p (s j n) -> p s j n", s=2, j=NPAGE)
        v_pages = half_b[:, :].rearrange("p (s j n) -> p s j n", s=2, j=NPAGE)
        ew_gate = [sb(f"ew_gate{u}", [P, KT, EF]) for u in range(2)]
        ew_up = [sb(f"ew_up{u}", [P, KT, EF]) for u in range(2)]
        ew_down = [sb(f"ew_down{u}", [P, FB, D]) for u in range(2)]
        xT = sb("xT", [P, KT, T])
        hT = sb("hT", [P, KT, T])
        zT = sb("zT", [P, 2 * KT, T])
        tokbuf = sb("tokbuf", [P, NT, D])
        sq = sb("sq", [P, KT, T])
        cst = sb("cst", [P, NCONST])
        ones = sb("ones", [P, P])
        mean_d = sb("mean_d", [P, P])
        mean_h = sb("mean_h", [P, P])
        eps = sb("eps", [P, 1])
        gain_rows = sb("gain_rows", [5 * KT + 2, P])
        gains = sb("gains", [P, 5 * KT + 2])
        std = sb("std", [P, 2, T])
        rec = sb("rec", [P, 2, T])
        ws_both = sb("ws_both", [P, 2, 4 * P])
        shared = sb("shared", [P, 1536])
        probT = sb("probT", [P, 2, 2 * P])
        wsS = sb("wsS", [TSA, 4, TSA])
        w_route = sb("w_route", [P, DEPTH, KT, R5])
        b_route = sb("b_route", [1, DEPTH, R5])
        pages = sb("pages", [1, NB * NPAGE], I32)
        lg = sb("lg", [P, NR, EP])
        cmp_ge = sb("cmp_ge", [P, NR, EP * EP])
        cmp_gt = sb("cmp_gt", [P, NR, EP * EP])
        rank = sb("rank", [P, NR, EP])
        top = sb("top", [P, NR])
        ex = sb("ex", [P, NR, EP])
        wsel = sb("wsel", [P, NR, EP])
        s_all = sb("s_all", [P, NR])
        s_two = sb("s_two", [P, NR])
        fac = sb("fac", [P, NT, EP])
        gates = sb("gates", [P, NT, NE])
        gatesT = sb("gatesT", [NE, T])
        gsel = sb("gsel", [NE, 2, T])
        qs = sb("qs", [P, NB * QC])
        stat = sb("stat", [P, 4, 2 * NH])
        dst = sb("dst", [P, 64])
        SnT = sb("SnT", [TSA, P])
        PnT = sb("PnT", [TSA, P])
        Sn = sb("Sn", [P, TSA])
        Pn = sb("Pn", [P, TSA])

        ws_in = ws_both[:, 0, :].rearrange("p (g s) -> p g s", g=4)
        wsT = ws_both[:, 1, :].rearrange("p (g s) -> p g s", g=4)
        PdT = ws_both[:, :, :].rearrange("p a (j c) -> p (a j) c", c=P)
        bs_row = shared[0:1, 0:4 * T].rearrange("p (g n) -> p g n", g=4)
        kts = shared[:, 0:1024].rearrange("p (s n) -> p s n", s=2)
        prob = shared[:, 1024:1536].rearrange("p (s n) -> p s n", s=2)
        cprod = shared[0:ROT, 0:2 * T].rearrange("p (s n) -> p s n", s=2)
        sprod = shared[0:ROT, 2 * T:4 * T].rearrange("p (s n) -> p s n", s=2)
        sq_flat = sq[:, :, :].rearrange("p k n -> p (k n)")
        ST = sq_flat[:, 0:NPAGE * P].rearrange("p (j c) -> p j c", j=NPAGE)
        Pd = sq_flat[:, NPAGE * P:2 * NPAGE * P]
        silu = zT[:, 0:FB, :]
        hid = zT[:, FB:2 * FB, :]
        ktok = tokbuf[:, :, 0:ROWK]
        vrow = tokbuf[:, :, ROWK:2 * ROWK]
        uT, vT = zT[:, 0:KT, :], zT[:, KT:2 * KT, :]

        ident = cst[:, cols["ident"]]
        keep_upper = cst[:, cols["keep_upper"]]
        causal_neg = cst[:, cols["causal_neg"]]
        cosT = cst[0:ROT, cols["cos"]]
        sinT = cst[0:ROT, cols["sin"]]
        rotate = cst[0:ROT, cols["rotate"]]
        own_causal = cst[0:TSA, cols["own_causal"]]
        own_neg = cst[:, cols["own_neg"]]
        earlier = cst[:, cols["earlier"]]
        later = cst[:, cols["later"]]
        spread = cst[0:TS, cols["spread"]]

        names = """x_in const_in small_in pages_in w_v_in w_u_in w_out_in w_q_in w_kv_in w_o_in
            fill prep prep_sb xt xt_sb squared meansq rooted recip normed
            z z_sb vtok vtok_sb mixed gated proj res chunk_out
            logits shifted exped routed gT gT_sb gsel_sb gb gu silued upped hid_sb down added dve_step
            qkv qkv_sb hsq hms hroot hrec hnormed rot rcos rsin roped kvt kvt_sb rows_out gathered
            ps pneg pexp pnorm pt pt_sb po po_sb
            kt kt_dve kt_act sc st_sb sn sn_sb snr S_up dstep dbias dexp dnorm dpt dpt_act dpt_dve pv pv_sb
            y y_sb y_out held""".split()
        S = {n: sem("s_" + n) for n in names}
        FROM_ONE = "upped hid_sb added kt sc kt_dve kt_act st_sb pv pv_sb".split()
        s_eg = [sem(f"s_eg{u}") for u in range(2)]
        s_eu = [sem(f"s_eu{u}") for u in range(2)]
        s_ed = [sem(f"s_ed{u}") for u in range(2)]
        s_k = [sem(f"s_k{u}") for u in range(2)]
        s_v = [sem(f"s_v{u}") for u in range(2)]

        NORMS = [(xT, 0, hT), (vT, 4 * KT, vT), (xT, 2 * KT, hT), (xT, KT, hT), (xT, 3 * KT, hT)]
        ADDS = KT * NE
        DSTEPS = 12

        def source_ready(eng, n, k):
            if n == 0:
                eng.wait_ge(S["xt_sb"], k + 1)
            elif n == 1:
                eng.wait_ge(S["z_sb"], k + 1)
            elif n == 2:
                eng.wait_ge(S["res"], k + 1)
            elif n == 3:
                eng.wait_ge(S["added"], 1 + ADDS - KT + k + 1)
            else:
                eng.wait_ge(S["res"], KT + k + 1)

        units = [(h, c) for h in range(NH) for c in range(CH)]
        NU = len(units)

        block = ctx.enter_context(nc.Block())

        @block.sync
        def _(sp):
            def load(dst, src, s):
                sp.dma_start(dst, src).then_inc(s, 16)

            def hold(s, value):
                sp.wait_ge(s, value)
                sp.sem_inc(S["held"], 1)

            load(tokbuf[:, 0:CH, :], t["x_prompt"].rearrange("a (c p) d -> p (a c) d", p=P), S["x_in"])
            load(tokbuf[0:TSA, CH, :], t["x_sample"].rearrange("b t d -> (b t) d"), S["x_in"])
            load(cst[:, :], t["consts"], S["const_in"])
            load(gain_rows[0:2 * KT, :], t["norm1"].rearrange("l (k p) -> (l k) p", p=P), S["small_in"])
            load(gain_rows[2 * KT:4 * KT, :], t["norm2"].rearrange("l (k p) -> (l k) p", p=P), S["small_in"])
            load(gain_rows[4 * KT:5 * KT, :], t["a_g_v"].rearrange("l (k p) -> (l k) p", p=P), S["small_in"])
            load(gain_rows[5 * KT:5 * KT + 1, :], t["b_q_norm"], S["small_in"])
            load(gain_rows[5 * KT + 1:5 * KT + 2, :], t["b_k_norm"], S["small_in"])
            load(ws_in, t["a_w_s"].rearrange("l g t s -> t (l g) s"), S["small_in"])
            w_in = t["a_w_in"][0].rearrange("(k p) n -> p k n", p=P)
            load(w_a, w_in[:, :, D:2 * D], S["w_v_in"])
            load(w_b, w_in[:, :, 0:D], S["w_u_in"])
            for c in range(CH):
                load(bs_row[:, :, c * P:(c + 1) * P], t["a_b_s"], S["small_in"])
            for b in range(NB):
                load(bs_row[:, :, TP + b * TS:TP + (b + 1) * TS], t["a_b_s"][:, :, 0:TS], S["small_in"])
            for l in range(DEPTH):
                load(w_route[:, l, :, 0:EP], t["moe_w_group"][l].rearrange("(k p) n -> p k n", p=P), S["small_in"])
                load(w_route[:, l, :, EP:R5], t["moe_w_router"][l].rearrange("(k p) n -> p k n", p=P), S["small_in"])
                load(b_route[:, l, 0:EP], t["moe_b_group"][l:l + 1, :], S["small_in"])
                load(b_route[:, l, EP:R5], t["moe_b_router"][l:l + 1, :], S["small_in"])
            load(pages[:, :], t["page_table"].rearrange("b (a n) -> a (b n)", a=1), S["pages_in"])

            def expert(l, e, u):
                for dst, name, s in ((ew_gate, "moe_w_gate", s_eg), (ew_up, "moe_w_up", s_eu), (ew_down, "moe_w_down", s_ed)):
                    load(dst[u][:, :, :], t[name][l, bass.ds(e, 1)].rearrange("a (k p) n -> p (a k) n", p=P), s[u])

            def experts(l):
                with sp.Fori(0, NE // 2 - 1) as i:
                    for u in range(2):
                        done = l * NE + 2 * i + u + 1
                        hold(S["gu"], FB * done)
                        hold(S["down"], KT * done)
                        expert(l, 2 * i + 2 + u, u)

            for u in range(2):
                expert(0, u, u)
            sp.wait_ge(S["z"], KT)
            load(w_a, t["a_w_out"][0].rearrange("(k p) n -> p k n", p=P), S["w_out_in"])
            w_qkv = t["b_w_qkv"][0].rearrange("(k p) n -> p k n", p=P)
            sp.wait_ge(S["z"], 2 * KT)
            load(w_b, w_qkv[:, :, 0:D], S["w_q_in"])
            sp.wait_ge(S["vtok_sb"], 2 * NT)
            sp.dma_start(o["chunk"].rearrange("l b t d -> (l b t) d"), tokbuf[0:TSA, CH, :]).then_inc(S["chunk_out"], 16)
            sp.wait_ge(S["proj"], KT)
            load(w_a, w_qkv[:, :, D:2 * D], S["w_kv_in"])
            experts(0)
            for u in range(2):
                sp.wait_ge(S["gu"], FB * (NE - 1 + u))
                sp.wait_ge(S["down"], KT * (NE - 1 + u))
                expert(1, u, u)
            sp.wait_ge(S["kvt_sb"], 2 * NT)
            for rows, src in (("kp", ktok), ("vp", vrow)):
                sp.dma_start(o[rows].rearrange("l a (c p) h d -> p (l a c) (h d)", p=P), src[:, 0:CH, :]).then_inc(S["rows_out"], 16)
            for rows, src in (("ks", ktok), ("vs", vrow)):
                sp.dma_start(o[rows].rearrange("l b t h d -> (l b t) (h d)"), src[0:TSA, CH, :]).then_inc(S["rows_out"], 16)
            sp.wait_ge(S["pages_in"], 16)
            sp.wait_ge(S["qkv"], 2 * KT)
            ck = t["cache_k"][0].rearrange("n p h d -> n p (h d)")
            cv = t["cache_v"][0].rearrange("n p h d -> n p (h d)")

            def sequence(b, dst, src, s):
                with sp.Fori(0, NPAGE) as j:
                    page = sp.value_load(pages[0:1, bass.ds(b * NPAGE + j, 1)], min_val=0, max_val=NPOOL - 1)
                    load(dst[:, bass.ds(j, 1), :], src[bass.ds(page, 1)].rearrange("a p n -> p a n"), s)

            with sp.Fori(0, NG) as g:
                for bb in range(GRP):
                    hold(S["kt"], 1 + (g * GRP + (bb - 1 if bb >= 2 else 0)) * NPAGE)
                    sequence(g * GRP + bb, k_pages[:, bb % 2], ck, s_k[bb % 2])
                for bb in range(GRP):
                    hold(S["pv"], 1 + g * GRP + (bb - 1 if bb >= 2 else 0))
                    sequence(g * GRP + bb, v_pages[:, bb % 2], cv, s_v[bb % 2])
            sp.wait_ge(S["kt"], 1 + NB * NPAGE)
            load(w_a, t["b_w_o"][0].rearrange("(k p) n -> p k n", p=P), S["w_o_in"])
            experts(1)
            sp.wait_ge(S["y_sb"], 2 * NT)
            sp.dma_start(o["yp"].rearrange("a (c p) d -> p (a c) d", p=P), tokbuf[:, 0:CH, :]).then_inc(S["y_out"], 16)
            sp.dma_start(o["ys"].rearrange("b t d -> (b t) d"), tokbuf[0:TSA, CH, :]).then_inc(S["y_out"], 16)
            sp.wait_ge(S["y_out"], 32)
            sp.wait_ge(S["rows_out"], 64)
            sp.wait_ge(S["chunk_out"], 16)

        @block.gpsimd
        def _(pool):
            for n in FROM_ONE:
                pool.sem_inc(S[n], 1)
            for tile, value in ((ones, 1.0), (mean_d, 1.0 / D), (mean_h, 1.0 / P), (eps, EPS)):
                pool.memset(tile[:, :], value).then_inc(S["fill"], 1)
            pool.memset(lg[:, :, :], 0.0).then_inc(S["fill"], 1)
            pool.wait_ge(S["const_in"], 16)
            for h in range(LH):
                pool.wait_ge(S["hnormed"], h + 1)
                if h >= 2:
                    pool.wait_ge(S["roped"], h - 1)
                pool.tensor_tensor(cprod[:, h % 2, :], zT[0:ROT, h, :], cosT, ALU.mult).then_inc(S["rcos"], 1)
            pool.wait_ge(S["roped"], NH)
            pool.tensor_copy(qs[:, :].rearrange("p (b h t) -> p b h t", b=NB, h=NH),
                             zT[:, 0:NH, TP:T].rearrange("p h (b t) -> p b h t", b=NB)).then_inc(S["gathered"], 1)

        @block.scalar
        def _(act):
            def squares(n):
                for k in range(KT):
                    source_ready(act, n, k)
                    act.activation(sq[:, k, :], NORMS[n][0][:, k, :], ACT.Square).then_inc(S["squared"], 1)

            def root(n):
                act.wait_ge(S["meansq"], n + 1)
                act.activation(std[:, 0, :], PS[:, 7, 0:T], ACT.Sqrt, bias=eps[:, :]).then_inc(S["rooted"], 1)

            def route(l):
                act.wait_ge(S["shifted"], l + 1)
                act.activation(ex[:, :, :], ex[:, :, :], ACT.Exp).then_inc(S["exped"], 1)

            def experts(l):
                with act.Fori(0, NE // 2) as i:
                    for u in range(2):
                        e = l * NE + 2 * i + u
                        for f in range(FB):
                            act.wait_ge(S["gu"], e * FB + f + 1)
                            act.activation(silu[:, f, :], PS[:, 2 * f, 0:T], ACT.Silu).then_inc(S["silued"], 1)

            act.wait_ge(S["fill"], 5)
            squares(0)
            root(0)
            for j in range(2 * KT):
                act.wait_ge(S["z"], j + 1)
                act.activation(zT[:, (j + KT) % (2 * KT), :], PS[:, j % 4, 0:T], ACT.Gelu_apprx_tanh).then_inc(S["z_sb"], 1)
                if j == KT - 1:
                    squares(1)
                if j == KT + 1:
                    root(1)
            squares(2)
            root(2)
            route(0)
            experts(0)
            squares(3)
            root(3)
            for i in range(LH + 1):
                if i < LH:
                    act.wait_ge(S["qkv_sb"], i + 1)
                    if i >= KT:
                        act.wait_ge(S["hms"], i - KT + 1)
                    act.activation(sq[:, i % KT, :], zT[:, i, :], ACT.Square).then_inc(S["hsq"], 1)
                if i >= 1:
                    h = i - 1
                    act.wait_ge(S["hms"], h + 1)
                    if h >= 2:
                        act.wait_ge(S["hrec"], h - 1)
                    act.activation(std[:, h % 2, :], PS[:, 4 + h % 2, 0:T], ACT.Sqrt, bias=eps[:, :]).then_inc(S["hroot"], 1)
            act.wait_ge(S["chunk_out"], 16)
            for i in range(2 * NT):
                _, n = tok[i % NT]
                act.wait_ge(S["kvt"], i + 1)
                act.copy((ktok, vrow)[i // NT][0:n, i % NT, :], PS[0:n, i % 4, :]).then_inc(S["kvt_sb"], 1)
            for i in range(NU + 2):
                if i < NU:
                    w = (units[i][1] + 1) * P
                    act.wait_ge(S["pneg"], i + 1)
                    if i >= 2:
                        act.wait_ge(S["pt"], i - 1)
                    act.activation(prob[:, i % 2, 0:w], PS[:, i % 2, 0:w], ACT.Exp, bias=stat[:, 1, i:i + 1],
                                   scale=SCALE, accum_out=stat[:, 2, i:i + 1]).then_inc(S["pexp"], 1)
                if i >= 2:
                    u = i - 2
                    w = (units[u][1] + 1) * P
                    act.wait_ge(S["pt"], u + 1)
                    if u >= 2:
                        act.wait_ge(S["po"], u - 1)
                    act.copy(probT[:, u % 2, 0:w], PS[:, 2 + u % 2, 0:w]).then_inc(S["pt_sb"], 1)
            with act.Fori(0, NG) as g:
                for n in range(1, GRP * NPAGE, 2):
                    act.wait_ge(S["kt"], 1 + g * (GRP * NPAGE) + n + 1)
                    act.wait_ge(S["sc"], 1 + g * (GRP * NPAGE) + (n - 1 if n >= 2 else 0))
                    act.copy(kts[:, 1, :], PS[:, 1, :]).then_inc(S["kt_act"], 1)
                act.wait_ge(S["dbias"], g + 1)
                for k in range(BLK):
                    w = slice(k * MOBA_BLOCK, (k + 1) * MOBA_BLOCK)
                    scores = PS[:, 6:8, :].rearrange("p a n -> p (a n)")
                    act.activation(Pd[:, w], scores[:, w], ACT.Exp, bias=dst[:, 16 + k:17 + k], scale=SCALE,
                                   accum_out=dst[:, 24 + k:25 + k]).then_inc(S["dexp"], 1)
                act.activation(Pn[:, :], Sn[:, :], ACT.Exp, bias=dst[:, 15:16], scale=SCALE,
                               accum_out=dst[:, 28:29]).then_inc(S["dexp"], 1)
                act.wait_ge(S["dpt"], g + 1)
                act.copy(PdT[:, 0:4, :].rearrange("p j c -> p (j c)"), PS[:, 0, :]).then_inc(S["dpt_act"], 1)
            squares(4)
            root(4)
            route(1)
            experts(1)
            act.wait_ge(S["rows_out"], 64)
            for i in range(2 * NT):
                _, n = tok[i // 2]
                act.wait_ge(S["y"], i + 1)
                act.copy(tokbuf[0:n, i // 2, (i % 2) * 512:(i % 2 + 1) * 512], PS[0:n, i % 4, :]).then_inc(S["y_sb"], 1)

        @block.vector
        def _(dve):
            chain = Chain(dve, S["dve_step"])

            def norm(n):
                src, col, dest = NORMS[n]
                dve.wait_ge(S["rooted"], n + 1)
                dve.reciprocal(rec[:, 0, :], std[:, 0, :]).then_inc(S["recip"], 1)
                dve.wait_ge(S["recip"], n + 1)
                for k in range(KT):
                    dve.scalar_tensor_tensor(out=dest[:, k, :], in0=src[:, k, :], scalar=gains[:, col + k:col + k + 1],
                                             in1=rec[:, 0, :], op0=ALU.mult, op1=ALU.mult).then_inc(S["normed"], 1)

            def project(first):
                for ob in range(KT):
                    dve.wait_ge(S["proj"], first + ob + 1)
                    dve.tensor_tensor(xT[:, ob, :], PS[:, 4 + ob % 3, 0:T], xT[:, ob, :], ALU.add).then_inc(S["res"], 1)

            def ranks(link, values, n):
                ge = cmp_ge[:, 0:n, :].rearrange("p r (j i) -> p r j i", j=EP)
                gt = cmp_gt[:, 0:n, :].rearrange("p r (j i) -> p r j i", j=EP)
                vi = values.unsqueeze(2).to_broadcast([P, n, EP, EP])
                vj = values.unsqueeze(3).to_broadcast([P, n, EP, EP])
                dve.tensor_tensor(ge, vi, vj, ALU.is_ge)
                link(dve.tensor_tensor(gt, vi, vj, ALU.is_gt))
                bc = [P, n, EP * EP]
                dve.tensor_tensor(cmp_ge[:, 0:n, :], cmp_ge[:, 0:n, :], earlier.unsqueeze(1).to_broadcast(bc), ALU.mult)
                link(dve.tensor_tensor(cmp_gt[:, 0:n, :], cmp_gt[:, 0:n, :], later.unsqueeze(1).to_broadcast(bc), ALU.mult))
                link(dve.tensor_tensor(cmp_ge[:, 0:n, :], cmp_ge[:, 0:n, :], cmp_gt[:, 0:n, :], ALU.add))
                link(dve.tensor_reduce(rank[:, 0:n, :], ge, AX.X, ALU.add))

            def route(l):
                link = chain.link
                dve.wait_ge(S["logits"], l + 1)
                pl = PS[:, 6, 0:NT * R5].rearrange("p (r n) -> p r n", n=EP)
                full = CH * R5 // EP
                dve.tensor_copy(lg[:, 0:full, :], pl[:, 0:full, :])
                link(dve.tensor_copy(lg[0:TSA, full:NR, :], pl[0:TSA, full:NR, :]))
                link(dve.tensor_reduce(top[:, :], lg[:, :, :], AX.X, ALU.max))
                dve.tensor_tensor(ex[:, :, :], lg[:, :, :], top[:, :].unsqueeze(2).to_broadcast([P, NR, EP]),
                                  ALU.subtract).then_inc(S["shifted"], 1)
                ranks(link, lg[:, :, :], NR)
                dve.wait_ge(S["exped"], l + 1)
                link(dve.scalar_tensor_tensor(out=wsel[:, :, :], in0=rank[:, :, :], scalar=2.0, in1=ex[:, :, :],
                                              op0=ALU.is_lt, op1=ALU.mult))
                dve.tensor_reduce(s_two[:, :], wsel[:, :, :], AX.X, ALU.add)
                link(dve.tensor_reduce(s_all[:, :], ex[:, :, :], AX.X, ALU.add))
                dve.reciprocal(s_two[:, :], s_two[:, :])
                link(dve.reciprocal(s_all[:, :], s_all[:, :]))
                two5 = s_two[:, :].rearrange("p (c r) -> p c r", c=NT)
                all5 = s_all[:, :].rearrange("p (c r) -> p c r", c=NT)
                rank5 = rank[:, :, :].rearrange("p (c r) n -> p c r n", c=NT)
                wsel5 = wsel[:, :, :].rearrange("p (c r) n -> p c r n", c=NT)
                link(dve.scalar_tensor_tensor(out=fac[:, :, :], in0=rank5[:, :, 0, :], scalar=1.0, in1=two5[:, :, 1:5],
                                              op0=ALU.is_lt, op1=ALU.mult))
                link(dve.tensor_tensor(fac[:, :, :], fac[:, :, :], all5[:, :, 0:1].to_broadcast([P, NT, EP]), ALU.mult))
                dve.tensor_tensor(gates[:, :, :].rearrange("p c (r n) -> p c r n", n=EP), wsel5[:, :, 1:5, :],
                                  fac[:, :, :].unsqueeze(3).to_broadcast([P, NT, EP, EP]), ALU.mult).then_inc(S["routed"], 1)
                dve.wait_ge(S["gT"], l + 1)
                dve.tensor_copy(gatesT[:, :], PS[0:NE, 7, 0:T]).then_inc(S["gT_sb"], 1)
                dve.wait_ge(S["gT_sb"], l + 1)

            def experts(l):
                with dve.Fori(0, NE // 2) as i:
                    for u in range(2):
                        e = l * NE + 2 * i + u
                        dve.tensor_scalar(gsel[:, u, :], gatesT[:, :], cst[0:NE, bass.ds(2 * i + u, 1)], None,
                                          ALU.mult).then_inc(S["gsel_sb"], 1)
                        for f in range(FB):
                            dve.wait_ge(S["silued"], e * FB + f + 1)
                            dve.tensor_tensor(silu[:, f, :], PS[:, 2 * f + 1, 0:T], silu[:, f, :], ALU.mult).then_inc(S["upped"], 1)
                            if f == 0:
                                dve.wait_ge(S["gb"], e + 1)
                            dve.wait_ge(S["upped"], 1 + e * FB + f + 1)
                            dve.tensor_tensor(hid[:, f, :], PS[:, 4, 0:T], silu[:, f, :], ALU.mult).then_inc(S["hid_sb"], 1)
                        dve.wait_ge(S["added"], 1 + e * KT)
                        for ob in range(KT):
                            dve.wait_ge(S["down"], e * KT + ob + 1)
                            dve.tensor_tensor(xT[:, ob, :], PS[:, 5 + ob % 2, 0:T], xT[:, ob, :], ALU.add).then_inc(S["added"], 1)

            def store_scores(base, bb):
                dve.wait_ge(S["sc"], 1 + base + (bb + 1) * NPAGE)
                dve.tensor_copy(ST[:, :, bb * QC:(bb + 1) * QC],
                                PS[:, 2 + bb % 2, 0:NPAGE * QC].rearrange("p (j c) -> p j c", j=NPAGE)).then_inc(S["st_sb"], 1)

            dve.wait_ge(S["prep"], 1)
            dve.tensor_copy(gains[:, :], PS[:, 6, 0:5 * KT + 2]).then_inc(S["prep_sb"], 1)
            for k in range(KT):
                dve.wait_ge(S["xt"], k + 1)
                dve.tensor_copy(xT[:, k, :], PS[:, k % 4, 0:T]).then_inc(S["xt_sb"], 1)
            dve.wait_ge(S["prep"], 2)
            dve.tensor_tensor(wsT, PS[:, 5, :].rearrange("p (g s) -> p g s", g=4),
                              keep_upper.unsqueeze(1).to_broadcast([P, 4, P]), ALU.mult).then_inc(S["prep_sb"], 1)
            dve.wait_ge(S["prep_sb"], 1)
            norm(0)
            dve.wait_ge(S["prep"], 3)
            corner = PS[0:TSA, 6, 0:4 * TS].rearrange("p (g t) -> p g t", g=4).unsqueeze(2).to_broadcast([TSA, 4, NB, TS])
            dve.tensor_tensor(wsS[:, :, :].rearrange("p g (b t) -> p g b t", b=NB), corner,
                              own_causal.rearrange("p (b t) -> p b t", b=NB).unsqueeze(1).to_broadcast([TSA, 4, NB, TS]),
                              ALU.mult).then_inc(S["prep_sb"], 1)
            norm(1)
            for i in range(2 * NT):
                _, n = tok[i // 2]
                dve.wait_ge(S["vtok"], i + 1)
                dve.tensor_copy(tokbuf[0:n, i // 2, (i % 2) * 512:(i % 2 + 1) * 512], PS[0:n, 4 + i % 2, :]).then_inc(S["vtok_sb"], 1)
            dve.wait_ge(S["z_sb"], 2 * KT)
            for j in range(KT):
                dve.wait_ge(S["mixed"], j + 1)
                dve.tensor_tensor(uT[:, j, :], PS[:, j % 4, 0:T], uT[:, j, :], ALU.mult).then_inc(S["gated"], 1)
            project(0)
            dve.wait_ge(S["res"], KT)
            norm(2)
            route(0)
            experts(0)
            dve.wait_ge(S["added"], 1 + ADDS)
            norm(3)
            for i in range(2 * KT + 1):
                if i < 2 * KT:
                    dve.wait_ge(S["qkv"], i + 1)
                    dve.tensor_copy(zT[:, i, :], PS[:, i % 4, 0:T]).then_inc(S["qkv_sb"], 1)
                h = i - 2
                if 0 <= h < LH:
                    col = 5 * KT + h // NH
                    dve.wait_ge(S["hroot"], h + 1)
                    dve.reciprocal(rec[:, h % 2, :], std[:, h % 2, :]).then_inc(S["hrec"], 1)
                    dve.wait_ge(S["hrec"], h + 1)
                    dve.wait_ge(S["hsq"], h + 1)
                    dve.scalar_tensor_tensor(out=zT[:, h, :], in0=zT[:, h, :], scalar=gains[:, col:col + 1],
                                             in1=rec[:, h % 2, :], op0=ALU.mult, op1=ALU.mult).then_inc(S["hnormed"], 1)
                h = i - 4
                if 0 <= h < LH:
                    dve.wait_ge(S["rot"], h + 1)
                    dve.tensor_tensor(sprod[:, h % 2, :], PS[0:ROT, 6 + h % 2, 0:T], sinT, ALU.mult).then_inc(S["rsin"], 1)
                    dve.wait_ge(S["rsin"], h + 1)
                    dve.wait_ge(S["rcos"], h + 1)
                    dve.tensor_tensor(zT[0:ROT, h, :], cprod[:, h % 2, :], sprod[:, h % 2, :], ALU.add).then_inc(S["roped"], 1)
            for i in range(NU + 3):
                if i < NU:
                    w = (units[i][1] + 1) * P
                    dve.wait_ge(S["ps"], i + 1)
                    chain.link(dve.tensor_reduce(stat[:, 0, i:i + 1], PS[:, i % 2, 0:w], AX.X, ALU.max))
                    dve.tensor_scalar(stat[:, 1, i:i + 1], stat[:, 0, i:i + 1], -SCALE, None, ALU.mult).then_inc(S["pneg"], 1)
                u = i - 1
                if 0 <= u < NU:
                    w = (units[u][1] + 1) * P
                    dve.wait_ge(S["pexp"], u + 1)
                    chain.link(dve.reciprocal(stat[:, 3, u:u + 1], stat[:, 2, u:u + 1]))
                    dve.tensor_scalar(prob[:, u % 2, 0:w], prob[:, u % 2, 0:w], stat[:, 3, u:u + 1], None,
                                      ALU.mult).then_inc(S["pnorm"], 1)
                u = i - 3
                if 0 <= u:
                    h, c = units[u]
                    dve.wait_ge(S["po"], u + 1)
                    dve.tensor_copy(hT[:, h, c * P:(c + 1) * P], PS[:, 4 + u % 2, 0:P]).then_inc(S["po_sb"], 1)
            with dve.Fori(0, NG) as g:
                base = g * (GRP * NPAGE)
                for n in range(0, GRP * NPAGE, 2):
                    dve.wait_ge(S["kt"], 1 + base + n + 1)
                    dve.wait_ge(S["sc"], 1 + base + (n - 1 if n >= 2 else 0))
                    dve.tensor_copy(kts[:, 0, :], PS[:, 0, :]).then_inc(S["kt_dve"], 1)
                    if n % NPAGE == 2 and n > NPAGE:
                        store_scores(base, n // NPAGE - 1)
                store_scores(base, GRP - 1)
                dve.wait_ge(S["sn"], g + 1)
                dve.tensor_copy(SnT[:, :], PS[0:TSA, 4, 0:P]).then_inc(S["sn_sb"], 1)
                dch = Chain(dve, S["dstep"], g * DSTEPS)
                link = dch.link
                scores = PS[:, 6:8, :].rearrange("p a (b n) -> p (a b) n", n=MOBA_BLOCK)
                dve.wait_ge(S["S_up"], g + 1)
                dve.tensor_reduce(dst[:, 4:8], scores, AX.X, ALU.max)
                link(dve.tensor_reduce(dst[:, 0:4], scores, AX.X, ALU.add))
                ranks(link, dst[:, 0:4].unsqueeze(1), 1)
                link(dve.tensor_scalar(dst[:, 8:12], rank[:, 0, :], TOP_BLOCKS - 0.5, NEG, ALU.is_gt, ALU.mult))
                dve.tensor_tensor(dst[:, 4:8], dst[:, 4:8], dst[:, 8:12], ALU.add)
                dve.wait_ge(S["snr"], g + 1)
                link(dve.tensor_tensor(Sn[:, :], PS[:, 5, 0:TSA], own_neg[:, bass.ds(g * TSA, TSA)], ALU.add))
                dve.tensor_reduce(dst[:, 12:13], dst[:, 4:8], AX.X, ALU.max)
                link(dve.tensor_reduce(dst[:, 13:14], Sn[:, :], AX.X, ALU.max))
                link(dve.tensor_tensor(dst[:, 14:15], dst[:, 12:13], dst[:, 13:14], ALU.max))
                link(dve.tensor_scalar(dst[:, 15:16], dst[:, 14:15], -SCALE, None, ALU.mult))
                dve.tensor_scalar(dst[:, 16:20], dst[:, 8:12], SCALE, dst[:, 15:16], ALU.mult, ALU.add).then_inc(S["dbias"], 1)
                dve.wait_ge(S["dexp"], (g + 1) * (BLK + 1))
                link(dve.tensor_reduce(dst[:, 32:33], dst[:, 24:29], AX.X, ALU.add))
                link(dve.reciprocal(dst[:, 33:34], dst[:, 32:33]))
                dve.tensor_scalar(Pn[:, :], Pn[:, :], dst[:, 33:34], None, ALU.mult).then_inc(S["dnorm"], 1)
                dve.tensor_scalar(Pd, Pd, dst[:, 33:34], None, ALU.mult).then_inc(S["dnorm"], 1)
                assert dch.n == DSTEPS, dch.n
                dve.wait_ge(S["dpt"], g + 1)
                dve.tensor_copy(PdT[:, 4:8, :].rearrange("p j c -> p (j c)"), PS[:, 1, :]).then_inc(S["dpt_dve"], 1)
                dve.tensor_copy(PnT[:, :], PS[0:TSA, 4, 0:P]).then_inc(S["dpt_dve"], 1)
                dve.wait_ge(S["pv"], 1 + (g + 1) * GRP)
                dve.tensor_copy(hT[:, :, bass.ds(TP + g * TG, TG)].rearrange("p h (b t) -> p h b t", b=GRP),
                                PS[:, 5, 0:P].rearrange("p (b h t) -> p h b t", b=GRP, h=NH)).then_inc(S["pv_sb"], 1)
            project(KT)
            dve.wait_ge(S["res"], 2 * KT)
            norm(4)
            route(1)
            experts(1)

        @block.tensor
        def _(pe):
            def mean_squares(n):
                for k in range(KT):
                    pe.wait_ge(S["squared"], n * KT + k + 1)
                    mm = pe.matmul(PS[:, 7, 0:T], mean_d[:, :], sq[:, k, :], start=(k == 0), stop=(k == KT - 1))
                mm.then_inc(S["meansq"], 1)

            def tiles(bank, w, col, src, s, ready=None):
                for k in range(KT):
                    if ready is not None:
                        pe.wait_ge(*ready(k))
                    mm = pe.matmul(PS[:, bank, 0:T], w[:, k, col:col + P], src[:, k, :], start=(k == 0), stop=(k == KT - 1))
                mm.then_inc(s, 1)

            def project(first, src, ready=None):
                for ob in range(KT):
                    if ob >= 3:
                        pe.wait_ge(S["res"], first + ob - 2)
                    tiles(4 + ob % 3, w_a, ob * P, src, S["proj"], ready if ob == 0 else None)

            def route(l):
                pe.wait_ge(S["normed"], ((2, 4)[l] + 1) * KT)
                for c, (at, n) in enumerate(tok):
                    out = PS[0:n, 6, c * R5:(c + 1) * R5]
                    pe.matmul(out, ones[0:1, 0:n], b_route[:, l, :], start=True, stop=False)
                    for k in range(KT):
                        mm = pe.matmul(out, hT[:, k, at:at + n], w_route[:, l, k, :], start=False, stop=(k == KT - 1))
                mm.then_inc(S["logits"], 1)
                pe.wait_ge(S["routed"], l + 1)
                for c, (at, n) in enumerate(tok):
                    mm = pe.transpose(PS[0:NE, 7, at:at + n], gates[0:n, c, :], ident[0:n, 0:n])
                mm.then_inc(S["gT"], 1)

            def experts(l):
                with pe.Fori(0, NE // 2) as i:
                    for u in range(2):
                        e = l * NE + 2 * i + u
                        arrived = 16 * (l * (NE // 2) + i + 1)
                        pe.wait_ge(s_eg[u], arrived)
                        pe.wait_ge(s_eu[u], arrived)
                        pe.wait_ge(S["upped"], 1 + e * FB)
                        for f in range(FB):
                            for bank, w in ((2 * f, ew_gate[u]), (2 * f + 1, ew_up[u])):
                                for k in range(KT):
                                    mm = pe.matmul(PS[:, bank, 0:T], w[:, k, f * P:(f + 1) * P], hT[:, k, :],
                                                   start=(k == 0), stop=(k == KT - 1))
                            mm.then_inc(S["gu"], 1)
                        pe.wait_ge(S["gsel_sb"], e + 1)
                        pe.wait_ge(S["hid_sb"], 1 + e * FB)
                        pe.matmul(PS[:, 4, 0:T], ones[0:NE, :], gsel[:, u, :], start=True, stop=True).then_inc(S["gb"], 1)
                        pe.wait_ge(s_ed[u], arrived)
                        pe.wait_ge(S["hid_sb"], 1 + (e + 1) * FB)
                        for ob in range(KT):
                            pe.wait_ge(S["added"], 1 + e * KT + (ob - 1 if ob >= 2 else 0))
                            for f in range(FB):
                                mm = pe.matmul(PS[:, 5 + ob % 2, 0:T], ew_down[u][:, f, ob * P:(ob + 1) * P], hid[:, f, :],
                                               start=(f == 0), stop=(f == FB - 1))
                            mm.then_inc(S["down"], 1)

            pe.wait_ge(S["const_in"], 16)
            pe.wait_ge(S["x_in"], 32)
            for k in range(KT):
                if k >= 4:
                    pe.wait_ge(S["xt_sb"], k - 3)
                for c, (at, n) in enumerate(tok):
                    mm = pe.transpose(PS[:, k % 4, at:at + n], tokbuf[0:n, c, k * P:(k + 1) * P], ident[0:n, 0:n])
                mm.then_inc(S["xt"], 1)
                if k == 3:
                    pe.wait_ge(S["small_in"], 16 * (6 + CH + NB + 4 * DEPTH))
                    pe.transpose(PS[:, 6, 0:5 * KT + 2], gain_rows[:, :], ident[0:5 * KT + 2, 0:5 * KT + 2]).then_inc(S["prep"], 1)
            for j in range(4):
                mm = pe.transpose(PS[:, 5, j * P:(j + 1) * P], ws_in[:, j, :], ident)
            mm.then_inc(S["prep"], 1)
            pe.wait_ge(S["fill"], 5)
            mean_squares(0)
            pe.wait_ge(S["prep_sb"], 2)
            pe.matmul(PS[0:TSA, 6, 0:4 * TS], spread, wsT[0:TS, :, 0:TS], start=True, stop=True).then_inc(S["prep"], 1)
            pe.wait_ge(S["w_v_in"], 16)
            for j in range(2 * KT):
                if j == KT:
                    pe.wait_ge(S["w_u_in"], 16)
                pe.wait_ge(S["z_sb"], j - 3) if j >= 4 else pe.wait_ge(S["xt_sb"], KT)
                tiles(j % 4, w_a if j < KT else w_b, (j % KT) * P, hT, S["z"],
                      (lambda k: (S["normed"], k + 1)) if j == 0 else None)
                if j == KT + 1:
                    mean_squares(1)
            pe.wait_ge(S["normed"], 2 * KT)
            pe.wait_ge(S["prep_sb"], 3)
            for i in range(2 * NT):
                at, n = tok[i // 2]
                if i >= 2:
                    pe.wait_ge(S["vtok_sb"], i - 1)
                for j in range(4):
                    mm = pe.transpose(PS[0:n, 4 + i % 2, j * P:(j + 1) * P], vT[:, (i % 2) * 4 + j, at:at + n], ident)
                mm.then_inc(S["vtok"], 1)
            pe.wait_ge(S["z_sb"], 2 * KT)
            pe.wait_ge(S["vtok_sb"], 2 * NT)
            for j in range(KT):
                q = j // (KT // 4)
                if j >= 4:
                    pe.wait_ge(S["gated"], j - 3)
                pe.matmul(PS[:, j % 4, 0:T], ones[0:1, :], bs_row[:, q, :], start=True, stop=True)
                for c, (at, n) in enumerate(tok):
                    w = wsT[:, q, :] if c < CH else wsS[:, q, :]
                    mm = pe.matmul(PS[:, j % 4, at:at + n], tokbuf[0:n, c, j * P:(j + 1) * P], w,
                                   start=False, stop=True, skip_group_check=True)
                mm.then_inc(S["mixed"], 1)
            pe.wait_ge(S["w_out_in"], 16)
            project(0, uT, lambda k: (S["gated"], k + 1))
            mean_squares(2)
            route(0)
            pe.wait_ge(S["gT_sb"], 1)
            experts(0)
            mean_squares(3)
            pe.wait_ge(S["w_q_in"], 16)
            for i in range(2 * KT):
                if i == KT:
                    pe.wait_ge(S["w_kv_in"], 16)
                if i >= 4:
                    pe.wait_ge(S["qkv_sb"], i - 3)
                tiles(i % 4, w_b if i < KT else w_a, (i % KT) * P, hT, S["qkv"],
                      (lambda k: (S["normed"], 3 * KT + k + 1)) if i == 0 else None)
                h = i - 1
                if 0 <= h < LH:
                    pe.wait_ge(S["hsq"], h + 1)
                    if h >= 2:
                        pe.wait_ge(S["hroot"], h - 1)
                    pe.matmul(PS[:, 4 + h % 2, 0:T], mean_h[:, :], sq[:, h % KT, :], start=True, stop=True).then_inc(S["hms"], 1)
                h = i - 3
                if 0 <= h < LH:
                    pe.wait_ge(S["hnormed"], h + 1)
                    if h >= 2:
                        pe.wait_ge(S["rsin"], h - 1)
                    pe.matmul(PS[0:ROT, 6 + h % 2, 0:T], rotate, zT[0:ROT, h, :], start=True, stop=True).then_inc(S["rot"], 1)
            pe.wait_ge(S["qkv_sb"], 2 * KT)
            pe.wait_ge(S["roped"], LH)
            for i in range(2 * NT):
                at, n = tok[i % NT]
                if i >= 4:
                    pe.wait_ge(S["kvt_sb"], i - 3)
                for a in range(KV):
                    mm = pe.transpose(PS[0:n, i % 4, a * P:(a + 1) * P], zT[:, NH + (i // NT) * KV + a, at:at + n], ident)
                mm.then_inc(S["kvt"], 1)
            pe.wait_ge(S["kvt_sb"], 2 * NT)
            for i in range(NU + 3):
                if i < NU:
                    h, c = units[i]
                    if i >= 2:
                        pe.wait_ge(S["pexp"], i - 1)
                    pe.matmul(PS[:, i % 2, 0:(c + 1) * P], zT[:, h, c * P:(c + 1) * P], zT[:, NH + h // G, 0:(c + 1) * P],
                              start=True, stop=True)
                    pe.matmul(PS[:, i % 2, c * P:(c + 1) * P], ident, causal_neg, start=False, stop=True,
                              skip_group_check=True).then_inc(S["ps"], 1)
                u = i - 2
                if 0 <= u < NU:
                    pe.wait_ge(S["pnorm"], u + 1)
                    if u >= 2:
                        pe.wait_ge(S["pt_sb"], u - 1)
                    for k in range(units[u][1] + 1):
                        mm = pe.transpose(PS[:, 2 + u % 2, k * P:(k + 1) * P], prob[:, u % 2, k * P:(k + 1) * P], ident)
                    mm.then_inc(S["pt"], 1)
                u = i - 3
                if 0 <= u:
                    h, c = units[u]
                    pe.wait_ge(S["pt_sb"], u + 1)
                    if u >= 2:
                        pe.wait_ge(S["po_sb"], u - 1)
                    for k in range(c + 1):
                        mm = pe.matmul(PS[:, 4 + u % 2, 0:P], vrow[:, k, (h // G) * P:(h // G + 1) * P],
                                       probT[:, u % 2, k * P:(k + 1) * P], start=(k == 0), stop=(k == c))
                    mm.then_inc(S["po"], 1)
            pe.wait_ge(S["po_sb"], NU)
            pe.wait_ge(S["gathered"], 1)
            with pe.Fori(0, NG) as g:
                base = g * (GRP * NPAGE)

                def copied(n, more):
                    pe.wait_ge(S["kt_act" if n % 2 else "kt_dve"], 1 + g * (GRP * NPAGE // 2) + n // 2 + more)

                for n in range(GRP * NPAGE + 1):
                    bb, j = divmod(n, NPAGE)
                    if n < GRP * NPAGE:
                        if j == 0:
                            pe.wait_ge(s_k[bb % 2], 16 * NPAGE * (2 * g + bb // 2 + 1))
                        copied(n, 0)
                        for a in range(KV):
                            mm = pe.transpose(PS[:, n % 2, a * P:(a + 1) * P], k_pages[:, bb % 2, j, a * P:(a + 1) * P], ident)
                        mm.then_inc(S["kt"], 1)
                    if n >= 1:
                        bb, j = divmod(n - 1, NPAGE)
                        if j == 0:
                            pe.wait_ge(S["st_sb"], 1 + g * GRP + (bb - 1 if bb >= 2 else 0))
                        copied(n - 1, 1)
                        for a in range(KV):
                            at = j * QC + a * G * TS
                            mm = pe.matmul(PS[:, 2 + bb % 2, at:at + G * TS], kts[:, (n - 1) % 2, a * P:(a + 1) * P],
                                           qs[:, bass.ds((g * GRP + bb) * QC + a * G * TS, G * TS)], start=True, stop=True)
                        mm.then_inc(S["sc"], 1)
                for a in range(KV):
                    for bb in range(GRP):
                        at = bb * QC + a * G * TS
                        mm = pe.matmul(PS[0:TSA, 4, at:at + G * TS], zT[:, NH + a, TP:T],
                                       qs[:, bass.ds(g * P + at, G * TS)], start=True, stop=True)
                mm.then_inc(S["sn"], 1)
                pe.wait_ge(S["sn_sb"], g + 1)
                pe.wait_ge(S["pv_sb"], 1 + g)
                pe.wait_ge(S["st_sb"], 1 + (g + 1) * GRP)
                for j in range(NPAGE):
                    mm = pe.transpose(PS[:, 6 + j // 4, (j % 4) * P:(j % 4 + 1) * P], ST[:, j, :], ident)
                mm.then_inc(S["S_up"], 1)
                pe.transpose(PS[:, 5, 0:TSA], SnT[:, :], ident[0:TSA, 0:TSA]).then_inc(S["snr"], 1)
                pe.wait_ge(S["dnorm"], 2 * (g + 1))
                for j in range(NPAGE):
                    pe.transpose(PS[:, j // 4, (j % 4) * P:(j % 4 + 1) * P], Pd[:, j * P:(j + 1) * P], ident)
                pe.transpose(PS[0:TSA, 4, 0:P], Pn[:, :], ident).then_inc(S["dpt"], 1)
                pe.wait_ge(S["dpt_act"], g + 1)
                pe.wait_ge(S["dpt_dve"], 2 * (g + 1))
                for bb in range(GRP):
                    pe.wait_ge(s_v[bb % 2], 16 * NPAGE * (2 * g + bb // 2 + 1))
                    for a in range(KV):
                        at = bb * QC + a * G * TS
                        out = PS[:, 5, at:at + G * TS]
                        for j in range(NPAGE):
                            pe.matmul(out, v_pages[:, bb % 2, j, a * P:(a + 1) * P], PdT[:, j, at:at + G * TS],
                                      start=(j == 0), stop=False)
                        mm = pe.matmul(out, vrow[0:TSA, CH, a * P:(a + 1) * P], PnT[:, at:at + G * TS], start=False, stop=True)
                    mm.then_inc(S["pv"], 1)
            pe.wait_ge(S["pv_sb"], 1 + NG)
            pe.wait_ge(S["w_o_in"], 16)
            project(KT, hT)
            mean_squares(4)
            route(1)
            pe.wait_ge(S["gT_sb"], 2)
            experts(1)
            pe.wait_ge(S["added"], 1 + 2 * ADDS)
            for i in range(2 * NT):
                at, n = tok[i // 2]
                if i >= 4:
                    pe.wait_ge(S["y_sb"], i - 3)
                for j in range(4):
                    mm = pe.transpose(PS[0:n, i % 4, j * P:(j + 1) * P], xT[:, (i % 2) * 4 + j, at:at + n], ident)
                mm.then_inc(S["y"], 1)


INPUTS = ["x_prompt", "x_sample", "cache_k", "cache_v", "page_table", "norm1", "norm2", "a_w_in", "a_g_v", "a_w_s",
          "a_b_s", "a_w_out", "b_w_qkv", "b_q_norm", "b_k_norm", "b_w_o", "moe_w_group", "moe_b_group",
          "moe_w_router", "moe_b_router", "moe_w_gate", "moe_w_up", "moe_w_down"]


def constants(TP, NB, TS, past):
    import numpy as np

    TSA = NB * TS
    T = TP + TSA
    cols, n = const_columns(T, TSA, TS)
    c = np.zeros((P, n), np.float32)
    row, col = np.arange(P)[:, None], np.arange(P)[None, :]
    c[:, cols["ident"]] = row == col
    c[:, cols["keep_upper"]] = row <= col
    c[:, cols["causal_neg"]] = np.where(col <= row, 0.0, NEG)
    half = ROT // 2
    pos = np.concatenate([np.arange(TP), np.tile(past + np.arange(TS), NB)]).astype(np.float32)
    inv = np.power(np.float32(THETA), -np.arange(half, dtype=np.float32) * np.float32(2.0) / np.float32(ROT))
    ang = inv[:, None].astype(np.float32) * pos[None, :]
    c[0:ROT, cols["cos"]] = np.tile(np.cos(ang), (2, 1))
    c[0:ROT, cols["sin"]] = np.tile(np.sin(ang), (2, 1))
    rotate = np.zeros((ROT, ROT), np.float32)
    for i in range(half):
        rotate[i + half, i] = -1.0
        rotate[i, i + half] = 1.0
    c[0:ROT, cols["rotate"]] = rotate
    r, q = np.arange(TSA)[:, None], np.arange(TSA)[None, :]
    c[0:TSA, cols["own_causal"]] = (r // TS == q // TS) & (r <= q)
    masks = []
    for g in range(NB // GRP):
        b, s = GRP * g + row // (NH * TS), row % TS
        masks.append(np.where((q // TS == b) & (q % TS <= s), 0.0, NEG))
    c[:, cols["own_neg"]] = np.concatenate(masks, 1)
    j, i = np.arange(16) // 4, np.arange(16) % 4
    c[:, cols["earlier"]] = i < j
    c[:, cols["later"]] = i > j
    c[0:TS, cols["spread"]] = np.arange(TS)[:, None] == q % TS
    return c


def kernel(**inputs):
    import numpy as np
    import concourse.bacc as bacc
    from concourse.bass_utils import run_bass_kernel_spmd

    nc = bacc.Bacc("TRN2", target_bir_lowering=False, num_devices=1)
    arrays, t = {}, {}
    for name in INPUTS:
        arrays[f"in_{name}"] = np.ascontiguousarray(inputs[name])
    _, TP, D = inputs["x_prompt"].shape
    NB, TS, _ = inputs["x_sample"].shape
    past = inputs["page_table"].shape[1] * inputs["cache_k"].shape[2]
    arrays["in_consts"] = constants(TP, NB, TS, past)
    for name in INPUTS + ["consts"]:
        a = arrays[f"in_{name}"]
        t[name] = nc.dram_tensor(f"in_{name}", a.shape, mybir.dt.from_np(a.dtype), kind="ExternalInput").ap()
    shapes = {"yp": (1, TP, D), "ys": (NB, TS, D), "kp": (1, 1, TP, KV, P), "vp": (1, 1, TP, KV, P),
              "ks": (1, NB, TS, KV, P), "vs": (1, NB, TS, KV, P), "chunk": (1, NB, TS, D)}
    o = {name: nc.dram_tensor(f"out_{name}", s, F32, kind="ExternalOutput").ap() for name, s in shapes.items()}
    hybrid_step(nc, t, o)
    r = run_bass_kernel_spmd(nc, [arrays], core_ids=[0])
    return tuple(r.results[0][f"out_{name}"] for name in shapes)
```

```python
from contextlib import ExitStack

import concourse.bass as bass
from concourse import mybir

F32 = mybir.dt.float32
I32 = mybir.dt.int32
BF16 = mybir.dt.bfloat16
ALU = mybir.AluOpType
ACT = mybir.ActivationFunctionType
AX = mybir.AxisListType

P = 128
EPS = 1e-6
NEG = -1e30
KV = 4
G = 2
NH = KV * G
ROT = 32
THETA = 500000.0
TOP_BLOCKS = 3
MOBA_BLOCK = 256
GRP = 4
SLOT = 64
HALF = 512


def const_columns(T, TSA, TS):
    at, out = 0, {}
    for name, n in (("ident", P), ("keep_upper", P), ("causal_neg", P), ("cos", T), ("sin", T),
                    ("rotate", ROT), ("own_causal", TSA), ("own_neg", TSA * TSA // (GRP * TS)),
                    ("earlier", 16), ("later", 16), ("spread", TSA), ("before", P), ("limits", 4),
                    ("expert_tri", 256), ("expert_slot", 16), ("extra_slot", 16), ("extra_items", 10),
                    ("evens", 5), ("first_items", 16), ("lanes", 2 * P), ("halves", 2), ("marks", 18)):
        out[name] = slice(at, at + n)
        at += n
    return out, at


class Chain:

    def __init__(self, eng, sem, base=0):
        self.eng, self.sem, self.base, self.n = eng, sem, base, 0

    def link(self, ins):
        self.n += 1
        ins.then_inc(self.sem, 1)
        self.eng.wait_ge(self.sem, self.base + self.n)


def hybrid_step(nc, t, o):
    D = t["x_prompt"].shape[2]
    TP = t["x_prompt"].shape[1]
    NB, TS = t["x_sample"].shape[0:2]
    TSA = NB * TS
    T = TP + TSA
    DEPTH = t["norm1"].shape[0]
    KT = D // P
    CH = TP // P
    NT = CH + 1
    NPAGE = t["page_table"].shape[1]
    NPOOL = t["cache_k"].shape[1]
    ROWK = KV * P
    NE = t["moe_w_gate"].shape[1]
    EF = t["moe_w_gate"].shape[3]
    FB = EF // P
    SCALE = float(P) ** -0.5
    NG = NB // GRP
    QC = NH * TS
    HR = GRP * G * TS
    BLK = NPAGE * P // MOBA_BLOCK
    EP = 4
    R5 = EP + NE
    NR = NT * R5 // EP
    LH = NH + KV
    TG = GRP * TS
    assert t["cache_k"].shape[2] == P and QC * GRP == P and DEPTH == 2 and NE == EP * EP and BLK == EP
    tok = [(c * P, P) for c in range(CH)] + [(TP, TSA)]
    cols, NCONST = const_columns(T, TSA, TS)

    with ExitStack() as ctx:
        def sb(name, shape, dt=F32):
            return ctx.enter_context(nc.sbuf_tensor(name, shape, dt))

        def sem(name):
            return ctx.enter_context(nc.semaphore(name))

        PS = ctx.enter_context(nc.psum_tensor("PS", [P, 8, 512], F32))

        half_a = sb("half_a", [P, KT * D])
        half_b = sb("half_b", [P, KT * D])
        w_a = half_a[:, :].rearrange("p (k n) -> p k n", k=KT)
        w_b = half_b[:, :].rearrange("p (k n) -> p k n", k=KT)
        k_pages = half_a[:, :].rearrange("p (s j n) -> p s j n", s=2, j=NPAGE)
        ew_in = [sb(f"ew_in{u}", [P, KT, 2, EF]) for u in range(2)]
        assert KT * 2 * EF == NPAGE * ROWK
        v_pages = [half_b[:, u * NPAGE * ROWK:(u + 1) * NPAGE * ROWK].rearrange("p (j n) -> p j n", j=NPAGE) for u in range(2)]
        v_pages += [ew_in[u][:, :, :, :].rearrange("p k f n -> p (k f n)").rearrange("p (j n) -> p j n", j=NPAGE) for u in range(2)]
        ew_down = [sb(f"ew_down{u}", [P, FB, D]) for u in range(2)]
        xT = sb("xT", [P, KT, T])
        hT = sb("hT", [P, KT, T])
        zT = sb("zT", [P, 2 * KT, T])
        tokbuf = sb("tokbuf", [P, NT, D])
        sq = sb("sq", [P, KT, T])
        cst = sb("cst", [P, NCONST])
        ones = sb("ones", [P, P])
        mean_d = sb("mean_d", [P, P])
        mean_h = sb("mean_h", [P, P])
        eps = sb("eps", [P, 1])
        spare = sb("spare", [P, 1])
        gain_rows = sb("gain_rows", [5 * KT + 2, P])
        gains = sb("gains", [P, 5 * KT + 2])
        std = sb("std", [P, 2, T])
        rec = sb("rec", [P, 2, T])
        ws_both = sb("ws_both", [P, 2, 4 * P])
        shared = sb("shared", [P, 1536])
        probT = sb("probT", [P, 2, 2 * P])
        wsS = sb("wsS", [TSA, 4, TSA])
        w_route = sb("w_route", [P, DEPTH, KT, R5])
        b_route = sb("b_route", [R5, DEPTH])
        pages = sb("pages", [1, NB * NPAGE], I32)
        lg = sb("lg", [P, NR, EP])
        cmp_ge = sb("cmp_ge", [P, NR, EP * EP])
        cmp_gt = sb("cmp_gt", [P, NR, EP * EP])
        rank = sb("rank", [P, NR, EP])
        top = sb("top", [P, NR])
        ex = sb("ex", [P, NR, EP])
        wsel = sb("wsel", [P, NR, EP])
        s_all = sb("s_all", [P, NR])
        s_two = sb("s_two", [P, NR])
        fac = sb("fac", [P, NT, EP])
        gates = sb("gates", [P, NT, NE])
        group_on = sb("group_on", [P, NT, EP])
        chosen = sb("chosen", [P, NT, 2, NE])
        chosen_any = sb("chosen_any", [P, NT, NE])
        pick = sb("pick", [P, NT, 2, NE])
        place = sb("place", [P, NT, NE])
        past_slot = sb("past_slot", [P, NT, NE])
        over = sb("over", [P, NE, 4])
        extra = sb("extra", [P, NE])
        tri = sb("tri", [P, NE * NE])
        extra_at = sb("extra_at", [P, NE])
        extra_off = sb("extra_off", [P, NE])
        slots = sb("slots", [P, NT, 2])
        gate2 = sb("gate2", [P, NT, 2])
        gate_rest = sb("gate_rest", [P, NT, 2])
        marks = sb("marks", [P, NT, 2, 6], BF16)
        lanes = sb("lanes", [P, 2 * P], BF16)
        late = tri[0:1, 0:10 * NE].rearrange("p (i e) -> p i e", i=10)
        late_n = sb("late_n", [1, 10])
        pairs_f = sb("pairs_f", [1, 8])
        items = sb("items", [1, NE + 10], I32)
        pairs = sb("pairs", [1, 1], I32)
        table = sb("table", [P, 2, 6])
        tok_off = sb("tok_off", [P, 4])
        row_idx = sb("row_idx", [P, 2], I32)
        this_out = sb("this_out", [P, 2], I32)
        next_out = sb("next_out", [P, 2], I32)
        next_gate = sb("next_gate", [P, 2])
        out_idx = [sb(f"out_idx{u}", [P, 1], I32) for u in range(2)]
        in_idx = [sb(f"in_idx{u}", [P, 1], I32) for u in range(2)]
        slot_gate = sb("slot_gate", [P, 2])
        qs = sb("qs", [P, NB * QC])
        stat = sb("stat", [P, 4, 2 * NH])
        dst = sb("dst", [P, 64])
        PnT = sb("PnT", [TSA, P])
        new_part = sb("new_part", [P, P])
        Sn = sb("Sn", [P, TSA])
        Pn = sb("Pn", [P, TSA])

        logitsT = std[0:R5, 1, :]
        ws_in = ws_both[:, 0, :].rearrange("p (g s) -> p g s", g=4)
        wsT = ws_both[:, 1, :].rearrange("p (g s) -> p g s", g=4)
        PdT = ws_both[:, :, :].rearrange("p a (j c) -> p (a j) c", c=P)
        bs_row = shared[0:1, 0:4 * T].rearrange("p (g n) -> p g n", g=4)
        prob = shared[:, 1024:1536].rearrange("p (s n) -> p s n", s=2)
        cprod = shared[0:ROT, 0:2 * T].rearrange("p (s n) -> p s n", s=2)
        sprod = shared[0:ROT, 2 * T:4 * T].rearrange("p (s n) -> p s n", s=2)
        sq_flat = sq[:, :, :].rearrange("p k n -> p (k n)")
        Pd = shared[:, 0:NPAGE * P]
        o_rows = Pd[:, 0:4 * P]
        z_all = zT[:, :, :].rearrange("p k n -> p (k n)")
        kts = [x[:, 0:4 * ROWK].rearrange("p (a n) -> p a n", a=KV) for x in (z_all, sq_flat)]
        v_heads = z_all[:, (NH + KV) * T:]
        q_pad = v_heads[:, 0:GRP * P].rearrange("p (b a c) -> p b a c", b=GRP, a=KV)
        q_all = v_heads[:, GRP * P:(GRP + 1) * P].rearrange("p (a b r) -> p a b r", a=KV, b=GRP)
        z_flat = zT[:, :, :].rearrange("p k n -> p (k n)")
        x_slots = z_flat[:, 0:1024].rearrange("p (u n) -> p u n", u=2)
        x_slotsT = z_flat[:, 1024:2048].rearrange("p (u j h n) -> p u j h n", u=2, j=4, h=2)
        y_slots = z_flat[:, 2048:3072].rearrange("p (u n) -> p u n", u=2)
        silu = z_flat[0:SLOT, 3072:3072 + EF]
        hid = z_flat[0:SLOT, 3328:3328 + EF]
        hidT = z_flat[:, 3584:3584 + FB * SLOT].rearrange("p (f n) -> p f n", f=FB)
        hot = z_flat[:, 3712:3712 + 6 * P].bitcast(BF16).rearrange("p (c k n) -> p c k n", c=NT, k=2)
        y_second = z_flat[:, 0:NT * D].rearrange("p (c n) -> p c n", c=NT)
        halves2 = (half_a, half_b)
        n_in, n_item = KT * 2 * EF, KT * 2 * EF + FB * D
        pre_in = [h[:, 0:n_in].rearrange("p (k f n) -> p k f n", k=KT, f=2) for h in halves2]
        pre_down = [h[:, n_in:n_item].rearrange("p (f n) -> p f n", f=FB) for h in halves2]
        x_rows = [half_a[:, n_item + c * D:n_item + (c + 1) * D] for c in range(2)] + [half_b[:, n_item:n_item + D]]
        h_dram = nc.dram_tensor("h_rows", [T, D], F32, kind="Internal").ap()
        y_dram = [nc.dram_tensor(f"y_rows{l}", [T, 2, D], F32, kind="Internal").ap() for l in range(DEPTH)]
        tok_tiles = [tokbuf[:, c, :] for c in range(NT)]
        ktok = tokbuf[:, :, 0:ROWK]
        vrow = tokbuf[:, :, ROWK:2 * ROWK]
        uT, vT = zT[:, 0:KT, :], zT[:, KT:2 * KT, :]

        ident = cst[:, cols["ident"]]
        keep_upper = cst[:, cols["keep_upper"]]
        causal_neg = cst[:, cols["causal_neg"]]
        cosT = cst[0:ROT, cols["cos"]]
        sinT = cst[0:ROT, cols["sin"]]
        rotate = cst[0:ROT, cols["rotate"]]
        own_causal = cst[0:TSA, cols["own_causal"]]
        own_neg = cst[:, cols["own_neg"]]
        earlier = cst[:, cols["earlier"]]
        later = cst[:, cols["later"]]
        spread = cst[0:TS, cols["spread"]]
        before = cst[:, cols["before"]]
        limits = cst[:, cols["limits"]]
        expert_tri = cst[:, cols["expert_tri"]]
        expert_slot = cst[:, cols["expert_slot"]]
        extra_slot = cst[:, cols["extra_slot"]]
        halves = cst[:, cols["halves"]]

        names = """x_in const_in small_in gains_in pages_in w_u_in w_out_in w_q_in w_kv_in w_o_in
            fill prep prep_sb xt xt_sb squared meansq rooted recip normed
            z z_sb vtok vtok_sb mixed gated proj res chunk_out
            logits biased logits_up shifted exped picked counted hrows hrows_sb ysum yt added dve_step
            xrows xrows_sb hrows_t
            qkv qkv_sb hsq hms hroot hrec hnormed rot rcos rsin roped kvt kvt_sb rows_out gathered
            ps pneg pexp pnorm pt pt_sb po po_sb
            kt kt_dve kt_act sc sn dstep dbias dexp dnorm dpt dpt_act dpt_dve pv pv_sb new_v o_sb ot q_set new_sb
            y_sum y_out held y_sum_pool""".split()
        S = {n: sem("s_" + n) for n in names}
        FROM_ONE = "kt sc kt_dve kt_act sn pv".split()
        E = [{n: sem(f"e{l}_{n}") for n in """step this slid planned xt xt_sb gu silued hid ht ht_sb dn y_sb hot tab idx out
              in0 in1 w0 w1 wd0 wd1 sc0 sc1""".split()} for l in range(DEPTH)]
        AHEAD = {"xt_sb": 2, "hid": 2, "ht_sb": 2, "y_sb": 2}
        s_wv = [sem(f"s_wv{half}") for half in range(2)]
        s_pre = [sem(f"s_pre{u}") for u in range(2)]
        s_yb = [sem(f"s_yb{c}") for c in range(NT)]
        s_k = [[sem(f"s_k{u}_{part}") for part in range(2)] for u in range(2)]
        s_v = [sem(f"s_v{u}") for u in range(GRP)]

        NORMS = [(xT, 0, hT), (vT, 4 * KT, vT), (xT, 2 * KT, hT), (xT, KT, hT), (xT, 3 * KT, hT)]
        ISTEPS = 4
        Y_ORDER = [KT - 1] + list(range(KT - 1))
        DSTEPS = 12

        def source_ready(eng, n, k):
            if n == 0:
                eng.wait_ge(S["xt_sb"], k + 1)
            elif n == 1:
                eng.wait_ge(S["z_sb"], k + 1)
            elif n == 2:
                eng.wait_ge(S["res"], k + 1)
            elif n == 3:
                eng.wait_ge(S["added"], Y_ORDER.index(k) + 1)
            else:
                eng.wait_ge(S["res"], KT + k + 1)

        ck = t["cache_k"][0].rearrange("n p h d -> n p (h d)")
        cv = t["cache_v"][0].rearrange("n p h d -> n p (h d)")

        def sequence(eng, b, dst, src, s, free=None):
            for part in range(2):
                pp = range(part * NPAGE // 2, (part + 1) * NPAGE // 2)
                if free is not None:
                    free(pp.stop)
                at = [eng.value_load(pages[0:1, bass.ds(b * NPAGE + j, 1)], min_val=0, max_val=NPOOL - 1) for j in pp]
                for j, page in zip(pp, at):
                    eng.dma_start(dst[:, j:j + 1, :], src[bass.ds(page, 1)].rearrange("a p n -> p a n")).then_inc(s[part], 16)

        units = [(h, c) for h in range(NH) for c in range(CH)]
        NU = len(units)

        block = ctx.enter_context(nc.Block())

        @block.sync
        def _(sp):
            def load(dst, src, s):
                sp.dma_start(dst, src).then_inc(s, 16)

            def hold(s, value):
                sp.wait_ge(s, value)
                sp.sem_inc(S["held"], 1)

            load(tokbuf[:, 0:CH, :], t["x_prompt"].rearrange("a (c p) d -> p (a c) d", p=P), S["x_in"])
            load(tokbuf[0:TSA, CH, :], t["x_sample"].rearrange("b t d -> (b t) d"), S["x_in"])
            load(cst[:, :], t["consts"], S["const_in"])
            load(gain_rows[0:2 * KT, :], t["norm1"].rearrange("l (k p) -> (l k) p", p=P), S["gains_in"])
            load(gain_rows[2 * KT:4 * KT, :], t["norm2"].rearrange("l (k p) -> (l k) p", p=P), S["gains_in"])
            load(gain_rows[4 * KT:5 * KT, :], t["a_g_v"].rearrange("l (k p) -> (l k) p", p=P), S["gains_in"])
            load(gain_rows[5 * KT:5 * KT + 1, :], t["b_q_norm"], S["gains_in"])
            load(gain_rows[5 * KT + 1:5 * KT + 2, :], t["b_k_norm"], S["gains_in"])
            load(ws_in, t["a_w_s"].rearrange("l g t s -> t (l g) s"), S["gains_in"])
            w_in = t["a_w_in"][0].rearrange("(k p) n -> p k n", p=P)
            for half in range(2):
                load(w_a[:, :, half * HALF:(half + 1) * HALF], w_in[:, :, D + half * HALF:D + (half + 1) * HALF], s_wv[half])
            load(w_b, w_in[:, :, 0:D], S["w_u_in"])
            for c in range(CH):
                load(bs_row[:, :, c * P:(c + 1) * P], t["a_b_s"], S["small_in"])
            for b in range(NB):
                load(bs_row[:, :, TP + b * TS:TP + (b + 1) * TS], t["a_b_s"][:, :, 0:TS], S["small_in"])
            for l in range(DEPTH):
                load(w_route[:, l, :, 0:EP], t["moe_w_group"][l].rearrange("(k p) n -> p k n", p=P), S["small_in"])
                load(w_route[:, l, :, EP:R5], t["moe_w_router"][l].rearrange("(k p) n -> p k n", p=P), S["small_in"])
                load(b_route[0:EP, l:l + 1], t["moe_b_group"][l:l + 1, :].rearrange("l n -> n l"), S["small_in"])
                load(b_route[EP:R5, l:l + 1], t["moe_b_router"][l:l + 1, :].rearrange("l n -> n l"), S["small_in"])
            load(pages[:, :], t["page_table"].rearrange("b (a n) -> a (b n)", a=1), S["pages_in"])

            def expert_in(l, e, dst, s):
                for f, name in enumerate(("moe_w_gate", "moe_w_up")):
                    load(dst[:, :, f, :], t[name][l, bass.ds(e, 1)].rearrange("a (k p) n -> p (a k) n", p=P), s)

            def expert_down(l, e, dst, s):
                load(dst[:, :, :], t["moe_w_down"][l, bass.ds(e, 1)].rearrange("a (k p) n -> p (a k) n", p=P), s)

            def prefetch(l, u):
                expert_in(l, 2 + u, pre_in[u], s_pre[u])
                expert_down(l, 2 + u, pre_down[u], s_pre[u])

            def experts(l):
                def item(e, u, before):
                    hold(E[l]["gu"], before + 1)
                    expert_in(l, e, ew_in[u], E[l][f"w{u}"])
                    hold(E[l]["dn"], before + 1)
                    expert_down(l, e, ew_down[u], E[l][f"wd{u}"])

                for u in range(2):
                    item(4 + u, u, u)
                sp.wait_ge(E[l]["planned"], 1)
                n = sp.value_load(pairs[0:1, 0:1], min_val=NE // 2, max_val=NE // 2 + 5)
                with sp.Fori(3, n) as i:
                    for u in range(2):
                        e = sp.value_load(items[0:1, bass.ds(2 * i + u, 1)], min_val=0, max_val=NE - 1)
                        item(e, u, 2 * i - 2 + u)
                for u in range(2):
                    hold(E[l][f"sc{u}"], 16 * n + 16)
                    hold(E[l][f"in{u}"], 16 * n + 16)
                hold(E[l]["xt_sb"], AHEAD["xt_sb"] + 2 * n + 1)
                for c, (at, m) in enumerate(tok):
                    for k, dst in enumerate((tokbuf, y_second)):
                        load(dst[0:m, c, :], y_dram[l][at:at + m, k, :], s_yb[c])

            for u in range(2):
                expert_in(0, u, ew_in[u], E[0][f"w{u}"])
                expert_down(0, u, ew_down[u], E[0][f"wd{u}"])
            sp.wait_ge(S["z"], KT)
            load(w_a, t["a_w_out"][0].rearrange("(k p) n -> p k n", p=P), S["w_out_in"])
            w_qkv = t["b_w_qkv"][0].rearrange("(k p) n -> p k n", p=P)
            sp.wait_ge(S["z"], 2 * KT)
            prefetch(0, 1)
            sp.wait_ge(S["vtok_sb"], 2 * NT)
            sp.dma_start(o["chunk"].rearrange("l b t d -> (l b t) d"), tokbuf[0:TSA, CH, :]).then_inc(S["chunk_out"], 16)
            sp.wait_ge(S["proj"], KT)
            prefetch(0, 0)
            experts(0)
            load(w_b, w_qkv[:, :, 0:D], S["w_q_in"])
            load(w_a, w_qkv[:, :, D:2 * D], S["w_kv_in"])
            for u in range(2):
                expert_down(1, u, ew_down[u], E[1][f"wd{u}"])
            sp.wait_ge(S["pages_in"], 16)
            hold(S["qkv"], 2 * KT)
            for b in range(2):
                sequence(sp, b, k_pages[:, b], ck, s_k[b])
            sp.wait_ge(S["kvt_sb"], 2 * NT)
            for rows, src in (("kp", ktok), ("vp", vrow)):
                sp.dma_start(o[rows].rearrange("l a (c p) h d -> p (l a c) (h d)", p=P), src[:, 0:CH, :]).then_inc(S["rows_out"], 16)
            for rows, src in (("ks", ktok), ("vs", vrow)):
                sp.dma_start(o[rows].rearrange("l b t h d -> (l b t) (h d)"), src[0:TSA, CH, :]).then_inc(S["rows_out"], 16)
            with sp.Fori(1, NB // 2) as pair:
                for u in range(2):
                    sequence(sp, 2 * pair + u, k_pages[:, u], ck, s_k[u],
                             lambda n: hold(S["kt"], 1 + (2 * pair + u - 2) * NPAGE + n))
            sp.wait_ge(S["kt"], 1 + NB * NPAGE)
            load(w_a, t["b_w_o"][0].rearrange("(k p) n -> p k n", p=P), S["w_o_in"])
            for u in range(2):
                sp.wait_ge(S["pv"], 1 + NB - 1 + u)
                expert_in(1, u, ew_in[u], E[1][f"w{u}"])
            prefetch(1, 1)
            sp.wait_ge(S["proj"], 2 * KT)
            prefetch(1, 0)
            experts(1)
            sp.wait_ge(S["y_sum"], 1)
            sp.wait_ge(S["y_sum_pool"], 1)
            sp.dma_start(o["yp"].rearrange("a (c p) d -> p (a c) d", p=P), tokbuf[:, 0:CH, :]).then_inc(S["y_out"], 16)
            sp.wait_ge(S["y_sum"], 2)
            sp.dma_start(o["ys"].rearrange("b t d -> (b t) d"), tokbuf[0:TSA, CH, :]).then_inc(S["y_out"], 16)
            sp.wait_ge(S["y_out"], 32)
            sp.wait_ge(S["rows_out"], 64)
            sp.wait_ge(S["chunk_out"], 16)

        @block.gpsimd
        def _(pool):
            for n in FROM_ONE:
                pool.sem_inc(S[n], 1)
            for l in range(DEPTH):
                for n, ahead in AHEAD.items():
                    pool.sem_inc(E[l][n], ahead)
            for tile, value in ((ones, 1.0), (mean_d, 1.0 / D), (mean_h, 1.0 / P), (eps, EPS)):
                pool.memset(tile[:, :], value).then_inc(S["fill"], 1)
            for tile in (lg, place, past_slot):
                pool.memset(tile[:, :, :], 0.0).then_inc(S["fill"], 1)
            pool.wait_ge(S["const_in"], 16)
            pool.tensor_copy(lanes[:, :], cst[:, cols["lanes"]]).then_inc(S["fill"], 1)
            pool.tensor_copy(marks[:, :, :, 0:3], cst[:, cols["marks"]].rearrange("p (c k n) -> p c k n", c=NT, k=2)).then_inc(S["fill"], 1)
            pool.tensor_copy(items[:, 0:NE], cst[0:1, cols["first_items"]]).then_inc(S["fill"], 1)

            def experts(l):
                def hold(s, value):
                    pool.wait_ge(s, value)
                    pool.sem_inc(S["held"], 1)

                def gather(u):
                    pool.indirect_dma_start(out=x_slots[:, u, :], out_offset=None, in_=h_dram.rearrange("t (h n) -> (t h) n", h=2),
                                            in_offset=bass.IndirectOffsetOnAxis(ap=in_idx[u][:, 0:1], axis=0),
                                            bounds_check=2 * T - 1, oob_is_err=False).then_inc(E[l][f"in{u}"], 16)

                pool.wait_ge(S["hrows_sb"], 2 * NT * (l + 1))
                pool.dma_start(h_dram[0:TP, :].rearrange("(c p) d -> p c d", p=P), tokbuf[:, 0:CH, :]).then_inc(E[l]["sc0"], 16)
                pool.dma_start(h_dram[TP:T, :], tokbuf[0:TSA, CH, :]).then_inc(E[l]["sc1"], 16)
                for u in range(2):
                    pool.wait_ge(E[l][f"sc{u}"], 16)
                pool.wait_ge(E[l]["idx"], 1)
                for u in range(2):
                    gather(u)
                pool.wait_ge(E[l]["planned"], 1)
                n = pool.value_load(pairs[0:1, 0:1], min_val=NE // 2, max_val=NE // 2 + 5)
                with pool.Fori(0, n) as i:
                    hold(E[l]["idx"], i + 2)
                    for u in range(2):
                        hold(E[l]["xt"], 2 * i + u + 1)
                        gather(u)
                    for u in range(2):
                        hold(E[l]["out"], 2 * i + u + 1)
                        hold(E[l]["y_sb"], AHEAD["y_sb"] + 2 * i + u + 1)
                        pool.indirect_dma_start(out=y_dram[l].rearrange("t k (h n) -> (t k h) n", h=2),
                                                out_offset=bass.IndirectOffsetOnAxis(ap=out_idx[u][:, 0:1], axis=0),
                                                in_=y_slots[:, u, :], in_offset=None,
                                                bounds_check=4 * T - 1, oob_is_err=False).then_inc(E[l][f"sc{u}"], 16)
                for u in range(2):
                    pool.wait_ge(E[l][f"in{u}"], 16 * n + 16)
                    pool.wait_ge(E[l][f"sc{u}"], 16 * n + 16)
                pool.sem_inc(S["held"], 1)

            experts(0)
            pool.wait_ge(S["pages_in"], 16)
            pool.wait_ge(S["w_q_in"], 16)
            pool.sem_inc(S["held"], 1)
            for b in range(2, GRP):
                sequence(pool, b, v_pages[b], cv, [s_v[b]] * 2)
            for h in range(LH):
                pool.wait_ge(S["hnormed"], h + 1)
                if h >= 2:
                    pool.wait_ge(S["roped"], h - 1)
                pool.tensor_tensor(cprod[:, h % 2, :], zT[0:ROT, h, :], cosT, ALU.mult).then_inc(S["rcos"], 1)
            pool.wait_ge(S["roped"], NH)
            pool.wait_ge(S["kvt"], 2 * NT)
            pool.memset(v_heads[:, 0:GRP * P], 0.0).then_inc(S["gathered"], 1)
            pool.tensor_copy(qs[:, :].rearrange("p (b h t) -> p b h t", b=NB, h=NH),
                             zT[:, 0:NH, TP:T].rearrange("p h (b t) -> p b h t", b=NB)).then_inc(S["gathered"], 1)
            pool.wait_ge(S["qkv"], KT)
            pool.sem_inc(S["held"], 1)
            for b in range(2):
                sequence(pool, b, v_pages[b], cv, [s_v[b]] * 2)
            pool.wait_ge(S["gathered"], 2)
            with pool.Fori(0, NG) as g:
                pool.wait_ge(S["sn"], 1 + g)
                pool.sem_inc(S["held"], 1)
                for bb in range(GRP):
                    q = qs[:, bass.ds((g * GRP + bb) * QC, QC)].rearrange("p (a r) -> p a r", a=KV)
                    pool.tensor_copy(q_pad[:, bb, :, bb * G * TS:(bb + 1) * G * TS], q).then_inc(S["q_set"], 1)
                    pool.tensor_copy(q_all[:, :, bb, :], q).then_inc(S["q_set"], 1)
            with pool.Fori(1, NG) as g:
                for bb in range(GRP):
                    pool.wait_ge(S["pv"], 1 + (g - 1) * GRP + bb + 1)
                    pool.sem_inc(S["held"], 1)
                    sequence(pool, g * GRP + bb, v_pages[bb], cv, [s_v[bb]] * 2)
            experts(1)
            pool.wait_ge(s_yb[1], 4 * 16)
            pool.wait_ge(S["xrows_sb"], 2 * NT)
            pool.tensor_tensor(tokbuf[:, 1, :], tokbuf[:, 1, :], y_second[:, 1, :], ALU.add).then_inc(S["ysum"], 1)
            pool.wait_ge(S["ysum"], 1)
            pool.tensor_tensor(tokbuf[:, 1, :], tokbuf[:, 1, :], x_rows[1], ALU.add).then_inc(S["y_sum_pool"], 1)

        @block.scalar
        def _(act):
            def ready_for(func):
                act.activation(spare[:, :], eps[:, :], func)

            def squares(n):
                ready_for(ACT.Sqrt)
                for k in range(KT):
                    source_ready(act, n, k)
                    act.activation(sq[:, k, :], NORMS[n][0][:, k, :], ACT.Square).then_inc(S["squared"], 1)

            def root(n):
                act.wait_ge(S["meansq"], n + 1)
                act.activation(std[:, 0, :], PS[:, 7, 0:T], ACT.Sqrt, bias=eps[:, :]).then_inc(S["rooted"], 1)

            def route(l):
                ready_for(ACT.Exp)
                act.wait_ge(S["shifted"], l + 1)
                act.activation(ex[:, :, :], ex[:, :, :], ACT.Exp).then_inc(S["exped"], 1)

            def rows(src_sem, base, dst, done):
                for i in range(2 * NT):
                    _, n = tok[i // 2]
                    act.wait_ge(S[src_sem], base + i + 1)
                    act.copy(dst[i // 2][0:n, (i % 2) * HALF:(i % 2 + 1) * HALF], PS[0:n, i % 4, :]).then_inc(S[done], 1)

            def experts(l):
                act.wait_ge(E[l]["planned"], 1)
                n = act.value_load(pairs[0:1, 0:1], min_val=NE // 2, max_val=NE // 2 + 5)
                with act.Fori(0, n) as i:
                    ready_for(ACT.Silu)
                    for u in range(2):
                        act.wait_ge(E[l]["gu"], 2 * i + u + 1)
                        act.activation(silu, PS[0:SLOT, 2 + u, 0:EF], ACT.Silu).then_inc(E[l]["silued"], 1)
                        act.wait_ge(E[l]["dn"], 2 * i + u + 1)
                        act.wait_ge(E[l][f"sc{u}"], 16 * i + 16)
                        act.copy(y_slots[:, u, :], PS[:, 5 + u, :]).then_inc(E[l]["y_sb"], 1)

            act.wait_ge(S["fill"], 5)
            squares(0)
            root(0)
            for j in range(2 * KT):
                act.wait_ge(S["z"], j + 1)
                act.activation(zT[:, (j + KT) % (2 * KT), :], PS[:, j % 4, 0:T], ACT.Gelu_apprx_tanh).then_inc(S["z_sb"], 1)
                if j == KT - 1:
                    squares(1)
                if j == KT + 1:
                    root(1)
            squares(2)
            root(2)
            route(0)
            act.wait_ge(S["chunk_out"], 16)
            rows("hrows", 0, tok_tiles, "hrows_sb")
            experts(0)
            squares(3)
            root(3)
            for i in range(LH + 1):
                if i < LH:
                    act.wait_ge(S["qkv_sb"], i + 1)
                    if i >= KT:
                        act.wait_ge(S["hms"], i - KT + 1)
                    act.activation(sq[:, i % KT, :], zT[:, i, :], ACT.Square).then_inc(S["hsq"], 1)
                if i >= 1:
                    h = i - 1
                    act.wait_ge(S["hms"], h + 1)
                    if h >= 2:
                        act.wait_ge(S["hrec"], h - 1)
                    act.activation(std[:, h % 2, :], PS[:, 4 + h % 2, 0:T], ACT.Sqrt, bias=eps[:, :]).then_inc(S["hroot"], 1)
            act.wait_ge(S["chunk_out"], 16)
            for i in range(2 * NT):
                _, n = tok[i % NT]
                act.wait_ge(S["kvt"], i + 1)
                act.copy((ktok, vrow)[i // NT][0:n, i % NT, :], PS[0:n, i % 4, :]).then_inc(S["kvt_sb"], 1)
            for i in range(NU + 2):
                if i < NU:
                    w = (units[i][1] + 1) * P
                    act.wait_ge(S["pneg"], i + 1)
                    if i >= 2:
                        act.wait_ge(S["pt"], i - 1)
                    act.activation(prob[:, i % 2, 0:w], PS[:, i % 2, 0:w], ACT.Exp, bias=stat[:, 1, i:i + 1],
                                   scale=SCALE, accum_out=stat[:, 2, i:i + 1]).then_inc(S["pexp"], 1)
                if i >= 2:
                    u = i - 2
                    w = (units[u][1] + 1) * P
                    act.wait_ge(S["pt"], u + 1)
                    if u >= 2:
                        act.wait_ge(S["po"], u - 1)
                    act.copy(probT[:, u % 2, 0:w], PS[:, 2 + u % 2, 0:w]).then_inc(S["pt_sb"], 1)
            with act.Fori(0, NG) as g:
                for n in range(1, GRP * NPAGE, 2):
                    half, j = divmod(n, 4)
                    act.wait_ge(S["kt"], 1 + g * (GRP * NPAGE) + n + 1)
                    act.wait_ge(S["sc"], 1 + g * (2 * GRP) + max(half - 1, 0))
                    act.copy(kts[half % 2][:, :, j * P:(j + 1) * P], PS[:, 1, :].rearrange("p (a n) -> p a n", a=KV)).then_inc(S["kt_act"], 1)
                act.wait_ge(S["dbias"], g + 1)
                for k in range(BLK):
                    w = slice(k * MOBA_BLOCK, (k + 1) * MOBA_BLOCK)
                    scores = PS[:, 6:8, :].rearrange("p a n -> p (a n)")
                    act.activation(Pd[:, w], scores[:, w], ACT.Exp, bias=dst[:, 16 + k:17 + k], scale=SCALE,
                                   accum_out=dst[:, 24 + k:25 + k]).then_inc(S["dexp"], 1)
                act.activation(Pn[:, :], Sn[:, :], ACT.Exp, bias=dst[:, 15:16], scale=SCALE,
                               accum_out=dst[:, 28:29]).then_inc(S["dexp"], 1)
                act.wait_ge(S["dpt"], g + 1)
                act.copy(PdT[:, 0:4, :].rearrange("p j c -> p (j c)"), PS[:, 0, :]).then_inc(S["dpt_act"], 1)
                act.wait_ge(S["pv"], 1 + (g + 1) * GRP)
                act.copy(o_rows, PS[:, 5, :]).then_inc(S["o_sb"], 1)
            squares(4)
            root(4)
            route(1)
            act.wait_ge(S["rows_out"], 64)
            rows("hrows", 2 * NT, tok_tiles, "hrows_sb")
            rows("xrows", 0, x_rows, "xrows_sb")
            experts(1)

        @block.vector
        def _(dve):
            chain = Chain(dve, S["dve_step"])

            def norm(n):
                src, col, dest = NORMS[n]
                dve.wait_ge(S["rooted"], n + 1)
                dve.reciprocal(rec[:, 0, :], std[:, 0, :]).then_inc(S["recip"], 1)
                dve.wait_ge(S["recip"], n + 1)
                for k in range(KT):
                    dve.scalar_tensor_tensor(out=dest[:, k, :], in0=src[:, k, :], scalar=gains[:, col + k:col + k + 1],
                                             in1=rec[:, 0, :], op0=ALU.mult, op1=ALU.mult).then_inc(S["normed"], 1)

            def project(first):
                for ob in range(KT):
                    dve.wait_ge(S["proj"], first + ob + 1)
                    dve.tensor_tensor(xT[:, ob, :], PS[:, 4 + ob % 3, 0:T], xT[:, ob, :], ALU.add).then_inc(S["res"], 1)

            def ranks(link, values, n):
                ge = cmp_ge[:, 0:n, :].rearrange("p r (j i) -> p r j i", j=EP)
                gt = cmp_gt[:, 0:n, :].rearrange("p r (j i) -> p r j i", j=EP)
                vi = values.unsqueeze(2).to_broadcast([P, n, EP, EP])
                vj = values.unsqueeze(3).to_broadcast([P, n, EP, EP])
                dve.tensor_tensor(ge, vi, vj, ALU.is_ge)
                link(dve.tensor_tensor(gt, vi, vj, ALU.is_gt))
                bc = [P, n, EP * EP]
                dve.tensor_tensor(cmp_ge[:, 0:n, :], cmp_ge[:, 0:n, :], earlier.unsqueeze(1).to_broadcast(bc), ALU.mult)
                link(dve.tensor_tensor(cmp_gt[:, 0:n, :], cmp_gt[:, 0:n, :], later.unsqueeze(1).to_broadcast(bc), ALU.mult))
                link(dve.tensor_tensor(cmp_ge[:, 0:n, :], cmp_ge[:, 0:n, :], cmp_gt[:, 0:n, :], ALU.add))
                link(dve.tensor_reduce(rank[:, 0:n, :], ge, AX.X, ALU.add))

            def route(l):
                link = chain.link
                dve.wait_ge(S["logits"], l + 1)
                dve.tensor_scalar(logitsT, PS[0:R5, 6, 0:T], b_route[:, l:l + 1], None, ALU.add).then_inc(S["biased"], 1)
                dve.wait_ge(S["logits_up"], l + 1)
                pl = PS[:, 5, 0:NT * R5].rearrange("p (r n) -> p r n", n=EP)
                full = CH * R5 // EP
                dve.tensor_copy(lg[:, 0:full, :], pl[:, 0:full, :])
                link(dve.tensor_copy(lg[0:TSA, full:NR, :], pl[0:TSA, full:NR, :]))
                link(dve.tensor_reduce(top[:, :], lg[:, :, :], AX.X, ALU.max))
                dve.tensor_tensor(ex[:, :, :], lg[:, :, :], top[:, :].unsqueeze(2).to_broadcast([P, NR, EP]),
                                  ALU.subtract).then_inc(S["shifted"], 1)
                ranks(link, lg[:, :, :], NR)
                dve.wait_ge(S["exped"], l + 1)
                link(dve.scalar_tensor_tensor(out=wsel[:, :, :], in0=rank[:, :, :], scalar=2.0, in1=ex[:, :, :],
                                              op0=ALU.is_lt, op1=ALU.mult))
                dve.tensor_reduce(s_two[:, :], wsel[:, :, :], AX.X, ALU.add)
                link(dve.tensor_reduce(s_all[:, :], ex[:, :, :], AX.X, ALU.add))
                dve.reciprocal(s_two[:, :], s_two[:, :])
                link(dve.reciprocal(s_all[:, :], s_all[:, :]))
                two5 = s_two[:, :].rearrange("p (c r) -> p c r", c=NT)
                all5 = s_all[:, :].rearrange("p (c r) -> p c r", c=NT)
                rank5 = rank[:, :, :].rearrange("p (c r) n -> p c r n", c=NT)
                wsel5 = wsel[:, :, :].rearrange("p (c r) n -> p c r n", c=NT)
                link(dve.scalar_tensor_tensor(out=fac[:, :, :], in0=rank5[:, :, 0, :], scalar=1.0, in1=two5[:, :, 1:5],
                                              op0=ALU.is_lt, op1=ALU.mult))
                link(dve.tensor_tensor(fac[:, :, :], fac[:, :, :], all5[:, :, 0:1].to_broadcast([P, NT, EP]), ALU.mult))
                four = [P, NT, EP, EP]
                link(dve.tensor_tensor(gates[:, :, :].rearrange("p c (r n) -> p c r n", n=EP), wsel5[:, :, 1:5, :],
                                       fac[:, :, :].unsqueeze(3).to_broadcast(four), ALU.mult))
                link(dve.tensor_scalar(group_on[:, :, :], rank5[:, :, 0, :], 1.0, None, ALU.is_lt))
                for k in range(2):
                    last = dve.scalar_tensor_tensor(out=chosen[:, :, k, :].rearrange("p c (r n) -> p c r n", n=EP),
                                                    in0=rank5[:, :, 1:5, :], scalar=float(k),
                                                    in1=group_on[:, :, :].unsqueeze(3).to_broadcast(four),
                                                    op0=ALU.is_equal, op1=ALU.mult)
                link(last)
                dve.tensor_tensor(chosen_any[:, :, :], chosen[:, :, 0, :], chosen[:, :, 1, :], ALU.add).then_inc(S["picked"], 1)
                dve.wait_ge(S["fill"], 10)
                two = [P, NT, 2, NE]
                link(dve.tensor_tensor(pick[:, :, :, :], chosen[:, :, :, :], gates[:, :, :].unsqueeze(2).to_broadcast(two), ALU.mult))
                link(dve.tensor_reduce(gate2[:, :, :], pick[:, :, :, :], AX.X, ALU.add))
                link(dve.tensor_copy(marks[:, :, :, 3], gate2[:, :, :]))
                link(dve.tensor_tensor(gate_rest[:, :, :], gate2[:, :, :], marks[:, :, :, 3], ALU.subtract))
                link(dve.tensor_copy(marks[:, :, :, 4], gate_rest[:, :, :]))
                link(dve.tensor_tensor(marks[:, :, :, 5], gate_rest[:, :, :], marks[:, :, :, 4], ALU.subtract))
                dve.wait_ge(S["counted"], l + 1)
                before_me = PS[:, 7, 0:NT * NE].rearrange("p (c n) -> p c n", c=NT)
                per_expert = PS[:, 7, NT * NE:(NT + 1) * NE]
                link(dve.tensor_tensor(over[:, :, :], per_expert.unsqueeze(2).to_broadcast([P, NE, 4]),
                                       limits.unsqueeze(1).to_broadcast([P, NE, 4]), ALU.is_gt))
                link(dve.tensor_reduce(extra[:, :], over[:, :, :], AX.X, ALU.add))
                link(dve.tensor_tensor(tri[:, :].rearrange("p (a b) -> p a b", a=NE), extra[:, :].unsqueeze(1).to_broadcast([P, NE, NE]),
                                       expert_tri.rearrange("p (a b) -> p a b", a=NE), ALU.mult))
                link(dve.tensor_reduce(extra_at[:, :], tri[:, :].rearrange("p (a b) -> p a b", a=NE), AX.X, ALU.add))
                link(dve.scalar_tensor_tensor(out=extra_off[:, :], in0=extra_at[:, :], scalar=float(SLOT), in1=extra_slot,
                                              op0=ALU.mult, op1=ALU.add))
                three = [P, NT, NE]
                for c, (_, m) in enumerate(tok):
                    dve.tensor_scalar(past_slot[0:m, c, :], before_me[0:m, c, :], SLOT - 0.5, None, ALU.is_gt)
                    last = dve.tensor_tensor(place[0:m, c, :], before_me[0:m, c, :], expert_slot[0:m, :], ALU.add)
                link(last)
                link(dve.tensor_tensor(past_slot[:, :, :], past_slot[:, :, :], extra_off[:, :].unsqueeze(1).to_broadcast(three), ALU.mult))
                link(dve.tensor_tensor(place[:, :, :], place[:, :, :], past_slot[:, :, :], ALU.add))
                link(dve.tensor_tensor(pick[:, :, :, :], chosen[:, :, :, :], place[:, :, :].unsqueeze(2).to_broadcast(two), ALU.mult))
                link(dve.tensor_reduce(slots[:, :, :], pick[:, :, :, :], AX.X, ALU.add))

            def one_hot(l, done):
                for c, (_, m) in enumerate(tok):
                    for k in range(2):
                        last = dve.tensor_scalar(hot[0:m, c, k, :], lanes[0:m, :], slots[0:m, c, k:k + 1], None, ALU.is_equal)
                last.then_inc(E[l]["hot"], 1)
                dve.wait_ge(E[l]["hot"], done)
                dve.tensor_scalar(slots[:, :, :], slots[:, :, :], -2.0 * SLOT, None, ALU.add).then_inc(E[l]["slid"], 1)

            def indices(l, at):
                tab = PS[:, 7, 0:16].rearrange("p (u n) -> p u n", u=2)
                step = Chain(dve, E[l]["step"], at)
                link = step.link
                link(dve.tensor_copy(table[:, :, :], tab[:, :, 0:6]))
                link(dve.scalar_tensor_tensor(out=tok_off[:, 0:2], in0=table[:, :, 0], scalar=-float(P), in1=table[:, :, 1],
                                              op0=ALU.mult, op1=ALU.add))
                for u in range(2):
                    last = dve.tensor_scalar(in_idx[u][:, :], tok_off[:, u:u + 1], 2.0, halves[:, 0:1], ALU.mult, ALU.add)
                last.then_inc(E[l]["idx"], 1)
                link(dve.scalar_tensor_tensor(out=tok_off[:, 2:4], in0=tok_off[:, 0:2], scalar=2.0, in1=table[:, :, 2],
                                              op0=ALU.mult, op1=ALU.add))
                dve.tensor_scalar(next_out[:, :], tok_off[:, 2:4], 2.0, halves[:, 1:2], ALU.mult, ALU.add)
                link(dve.tensor_reduce(next_gate[:, :], table[:, :, 3:6], AX.X, ALU.add))
                assert step.n == ISTEPS

            def plan(l):
                link = chain.link
                link(dve.tensor_tensor(extra_at[:, :], extra_at[:, :], extra[:, :], ALU.add))
                link(dve.tensor_tensor(late[:, :, :], extra_at[0:1, :].unsqueeze(1).to_broadcast([1, 10, NE]),
                                       cst[0:1, cols["extra_items"]].unsqueeze(2).to_broadcast([1, 10, NE]), ALU.is_le))
                dve.tensor_reduce(late_n[:, :], late[:, :, :], AX.X, ALU.add)
                link(dve.tensor_scalar(pairs_f[:, 0:5], cst[0:1, cols["evens"]], extra_at[0:1, NE - 1:NE], None, ALU.is_lt))
                link(dve.tensor_reduce(pairs_f[:, 5:6], pairs_f[:, 0:5], AX.X, ALU.add))
                dve.tensor_scalar(items[:, NE:NE + 10], late_n[:, :], float(NE - 1), None, ALU.min)
                dve.tensor_scalar(pairs[:, :], pairs_f[:, 5:6], float(NE // 2), None, ALU.add).then_inc(E[l]["planned"], 1)
                dve.wait_ge(E[l]["planned"], 1)

            def experts(l):
                el = E[l]

                def x_tile(u, done):
                    dve.wait_ge(el["xt"], done)
                    dve.tensor_copy(x_slotsT[:, u], PS[:, u, :].rearrange("p (j h n) -> p j h n", j=4, h=2)).then_inc(el["xt_sb"], 1)

                one_hot(l, 1)
                dve.wait_ge(el["tab"], 1)
                indices(l, 0)
                plan(l)
                n = dve.value_load(pairs[0:1, 0:1], min_val=NE // 2, max_val=NE // 2 + 5)
                x_tile(0, 1)
                with dve.Fori(0, n) as i:
                    dve.tensor_copy(this_out[:, :], next_out[:, :])
                    dve.tensor_copy(slot_gate[:, :], next_gate[:, :]).then_inc(el["this"], 1)
                    dve.wait_ge(el["this"], i + 1)
                    dve.wait_ge(el["tab"], i + 1)
                    dve.wait_ge(el["slid"], i + 1)
                    one_hot(l, i + 2)
                    for u in range(2):
                        q = 2 * i + u
                        dve.wait_ge(el["silued"], q + 1)
                        dve.scalar_tensor_tensor(out=hid, in0=PS[SLOT:2 * SLOT, 2 + u, 0:EF], scalar=slot_gate[0:SLOT, u:u + 1],
                                                 in1=silu, op0=ALU.mult, op1=ALU.mult).then_inc(el["hid"], 1)
                        x_tile(1 - u, q + 2)
                        dve.wait_ge(el["ht"], q + 1)
                        dve.tensor_copy(hidT, PS[:, 4, 0:FB * SLOT].rearrange("p (f n) -> p f n", f=FB)).then_inc(el["ht_sb"], 1)
                        dve.wait_ge(el[f"sc{u}"], 16 * i + 16)
                        dve.tensor_copy(out_idx[u][:, :], this_out[:, u:u + 1]).then_inc(el["out"], 1)
                        if u == 0:
                            dve.wait_ge(el["tab"], i + 2)
                            for v in range(2):
                                dve.wait_ge(el[f"in{v}"], 16 * i + 16)
                            indices(l, ISTEPS * (i + 1))
                    dve.wait_ge(el["out"], 2 * i + 2)

            dve.wait_ge(S["prep"], 1)
            dve.tensor_copy(gains[:, :], PS[:, 6, 0:5 * KT + 2]).then_inc(S["prep_sb"], 1)
            for k in range(KT):
                dve.wait_ge(S["xt"], k + 1)
                dve.tensor_copy(xT[:, k, :], PS[:, k % 4, 0:T]).then_inc(S["xt_sb"], 1)
            dve.wait_ge(S["prep"], 2)
            dve.tensor_tensor(wsT, PS[:, 5, :].rearrange("p (g s) -> p g s", g=4),
                              keep_upper.unsqueeze(1).to_broadcast([P, 4, P]), ALU.mult).then_inc(S["prep_sb"], 1)
            dve.wait_ge(S["prep_sb"], 1)
            norm(0)
            dve.wait_ge(S["prep"], 3)
            corner = PS[0:TSA, 6, 0:4 * TS].rearrange("p (g t) -> p g t", g=4).unsqueeze(2).to_broadcast([TSA, 4, NB, TS])
            dve.tensor_tensor(wsS[:, :, :].rearrange("p g (b t) -> p g b t", b=NB), corner,
                              own_causal.rearrange("p (b t) -> p b t", b=NB).unsqueeze(1).to_broadcast([TSA, 4, NB, TS]),
                              ALU.mult).then_inc(S["prep_sb"], 1)
            norm(1)
            for i in range(2 * NT):
                _, n = tok[i // 2]
                dve.wait_ge(S["vtok"], i + 1)
                dve.tensor_copy(tokbuf[0:n, i // 2, (i % 2) * 512:(i % 2 + 1) * 512], PS[0:n, 4 + i % 2, :]).then_inc(S["vtok_sb"], 1)
            dve.wait_ge(S["z_sb"], 2 * KT)
            for j in range(KT):
                dve.wait_ge(S["mixed"], j + 1)
                dve.tensor_tensor(uT[:, j, :], PS[:, j % 4, 0:T], uT[:, j, :], ALU.mult).then_inc(S["gated"], 1)
            project(0)
            dve.wait_ge(S["res"], KT)
            norm(2)
            route(0)
            experts(0)
            for c, (_, m) in enumerate(tok):
                dve.wait_ge(s_yb[c], 2 * 16)
                dve.tensor_tensor(tokbuf[0:m, c, :], tokbuf[0:m, c, :], y_second[0:m, c, :], ALU.add).then_inc(S["yt"], 1)
            for i, k in enumerate(Y_ORDER):
                dve.wait_ge(S["hrows_t"], i + 1)
                dve.tensor_tensor(xT[:, k, :], PS[:, k, 0:T], xT[:, k, :], ALU.add).then_inc(S["added"], 1)
            dve.wait_ge(S["added"], KT)
            norm(3)
            for i in range(2 * KT + 1):
                if i < 2 * KT:
                    dve.wait_ge(S["qkv"], i + 1)
                    dve.tensor_copy(zT[:, i, :], PS[:, i % 4, 0:T]).then_inc(S["qkv_sb"], 1)
                h = i - 2
                if 0 <= h < LH:
                    col = 5 * KT + h // NH
                    dve.wait_ge(S["hroot"], h + 1)
                    dve.reciprocal(rec[:, h % 2, :], std[:, h % 2, :]).then_inc(S["hrec"], 1)
                    dve.wait_ge(S["hrec"], h + 1)
                    dve.wait_ge(S["hsq"], h + 1)
                    dve.scalar_tensor_tensor(out=zT[:, h, :], in0=zT[:, h, :], scalar=gains[:, col:col + 1],
                                             in1=rec[:, h % 2, :], op0=ALU.mult, op1=ALU.mult).then_inc(S["hnormed"], 1)
                h = i - 4
                if 0 <= h < LH:
                    dve.wait_ge(S["rot"], h + 1)
                    dve.tensor_tensor(sprod[:, h % 2, :], PS[0:ROT, 6 + h % 2, 0:T], sinT, ALU.mult).then_inc(S["rsin"], 1)
                    dve.wait_ge(S["rsin"], h + 1)
                    dve.wait_ge(S["rcos"], h + 1)
                    dve.tensor_tensor(zT[0:ROT, h, :], cprod[:, h % 2, :], sprod[:, h % 2, :], ALU.add).then_inc(S["roped"], 1)
            for i in range(NU + 3):
                if i < NU:
                    w = (units[i][1] + 1) * P
                    dve.wait_ge(S["ps"], i + 1)
                    chain.link(dve.tensor_reduce(stat[:, 0, i:i + 1], PS[:, i % 2, 0:w], AX.X, ALU.max))
                    dve.tensor_scalar(stat[:, 1, i:i + 1], stat[:, 0, i:i + 1], -SCALE, None, ALU.mult).then_inc(S["pneg"], 1)
                u = i - 1
                if 0 <= u < NU:
                    w = (units[u][1] + 1) * P
                    dve.wait_ge(S["pexp"], u + 1)
                    chain.link(dve.reciprocal(stat[:, 3, u:u + 1], stat[:, 2, u:u + 1]))
                    dve.tensor_scalar(prob[:, u % 2, 0:w], prob[:, u % 2, 0:w], stat[:, 3, u:u + 1], None,
                                      ALU.mult).then_inc(S["pnorm"], 1)
                u = i - 3
                if 0 <= u:
                    h, c = units[u]
                    dve.wait_ge(S["po"], u + 1)
                    dve.tensor_copy(hT[:, h, c * P:(c + 1) * P], PS[:, 4 + u % 2, 0:P]).then_inc(S["po_sb"], 1)
            with dve.Fori(0, NG) as g:
                for n in range(0, GRP * NPAGE, 2):
                    half, j = divmod(n, 4)
                    dve.wait_ge(S["kt"], 1 + g * (GRP * NPAGE) + n + 1)
                    dve.wait_ge(S["sc"], 1 + g * (2 * GRP) + max(half - 1, 0))
                    dve.tensor_copy(kts[half % 2][:, :, j * P:(j + 1) * P], PS[:, 0, :].rearrange("p (a n) -> p a n", a=KV)).then_inc(S["kt_dve"], 1)
                dch = Chain(dve, S["dstep"], g * DSTEPS)
                link = dch.link
                scores = PS[:, 6:8, :].rearrange("p a (b n) -> p (a b) n", n=MOBA_BLOCK)
                dve.wait_ge(S["sc"], 1 + (g + 1) * 2 * GRP)
                dve.tensor_reduce(dst[:, 4:8], scores, AX.X, ALU.max)
                link(dve.tensor_reduce(dst[:, 0:4], scores, AX.X, ALU.add))
                ranks(link, dst[:, 0:4].unsqueeze(1), 1)
                link(dve.tensor_scalar(dst[:, 8:12], rank[:, 0, :], TOP_BLOCKS - 0.5, NEG, ALU.is_gt, ALU.mult))
                dve.tensor_tensor(dst[:, 4:8], dst[:, 4:8], dst[:, 8:12], ALU.add)
                dve.wait_ge(S["sn"], 1 + g + 1)
                link(dve.tensor_tensor(Sn[:, :], PS[:, 4, 0:TSA], own_neg[:, bass.ds(g * TSA, TSA)], ALU.add))
                dve.tensor_reduce(dst[:, 12:13], dst[:, 4:8], AX.X, ALU.max)
                link(dve.tensor_reduce(dst[:, 13:14], Sn[:, :], AX.X, ALU.max))
                link(dve.tensor_tensor(dst[:, 14:15], dst[:, 12:13], dst[:, 13:14], ALU.max))
                link(dve.tensor_scalar(dst[:, 15:16], dst[:, 14:15], -SCALE, None, ALU.mult))
                dve.tensor_scalar(dst[:, 16:20], dst[:, 8:12], SCALE, dst[:, 15:16], ALU.mult, ALU.add).then_inc(S["dbias"], 1)
                dve.wait_ge(S["dexp"], (g + 1) * (BLK + 1))
                link(dve.tensor_reduce(dst[:, 32:33], dst[:, 24:29], AX.X, ALU.add))
                link(dve.reciprocal(dst[:, 33:34], dst[:, 32:33]))
                dve.tensor_scalar(Pn[:, :], Pn[:, :], dst[:, 33:34], None, ALU.mult).then_inc(S["dnorm"], 1)
                dve.tensor_scalar(Pd, Pd, dst[:, 33:34], None, ALU.mult).then_inc(S["dnorm"], 1)
                assert dch.n == DSTEPS, dch.n
                dve.wait_ge(S["dpt"], g + 1)
                dve.tensor_copy(PdT[:, 4:8, :].rearrange("p j c -> p (j c)"), PS[:, 1, :]).then_inc(S["dpt_dve"], 1)
                dve.tensor_copy(PnT[:, :], PS[0:TSA, 4, 0:P]).then_inc(S["dpt_dve"], 1)
                dve.wait_ge(S["new_v"], g + 1)
                dve.tensor_copy(new_part[:, :], PS[:, 3, 0:P]).then_inc(S["new_sb"], 1)
                dve.wait_ge(S["new_sb"], g + 1)
                dve.wait_ge(S["ot"], g + 1)
                for bb in range(GRP):
                    past = PS[:, 2, bb * P:(bb + 1) * P].rearrange("p (a b g t) -> p b a g t", a=KV, b=GRP, g=G)[:, bb]
                    new = new_part[:, :].rearrange("p (a b g t) -> p b a g t", a=KV, b=GRP, g=G)[:, bb]
                    dve.tensor_tensor(hT[:, :, bass.ds(TP + g * TG + bb * TS, TS)].rearrange("p (a g) t -> p a g t", a=KV),
                                      past, new, ALU.add).then_inc(S["pv_sb"], 1)
            project(KT)
            dve.wait_ge(S["res"], 2 * KT)
            norm(4)
            route(1)
            experts(1)
            dve.wait_ge(S["xrows_sb"], 2 * NT)
            for c, (_, m) in ((0, tok[0]), (CH, tok[CH])):
                dve.wait_ge(s_yb[c], 4 * 16)
                chain.link(dve.tensor_tensor(tokbuf[0:m, c, :], tokbuf[0:m, c, :], y_second[0:m, c, :], ALU.add))
                dve.tensor_tensor(tokbuf[0:m, c, :], tokbuf[0:m, c, :], x_rows[c][0:m, :], ALU.add).then_inc(S["y_sum"], 1)

        @block.tensor
        def _(pe):
            def mean_squares(n, which=range(KT)):
                for k in which:
                    pe.wait_ge(S["squared"], n * KT + k + 1)
                    mm = pe.matmul(PS[:, 7, 0:T], mean_d[:, :], sq[:, k, :], start=(k == 0), stop=(k == KT - 1))
                    if k == KT - 1:
                        mm.then_inc(S["meansq"], 1)

            def tiles(bank, w, col, src, s, ready=None):
                for k in range(KT):
                    if ready is not None:
                        pe.wait_ge(*ready(k))
                    mm = pe.matmul(PS[:, bank, 0:T], w[:, k, col:col + P], src[:, k, :], start=(k == 0), stop=(k == KT - 1))
                mm.then_inc(s, 1)

            def project(first, src, n, ready=None):
                for ob in range(KT):
                    if ob >= 3:
                        pe.wait_ge(S["res"], first + ob - 2)
                    tiles(4 + ob % 3, w_a, ob * P, src, S["proj"], ready if ob == 0 else None)
                    if ob >= 3:
                        mean_squares(n, [ob - 3])
                mean_squares(n, range(KT - 3, KT))

            def route(l):
                for k in range(KT):
                    pe.wait_ge(S["normed"], (2, 4)[l] * KT + k + 1)
                    mm = pe.matmul(PS[0:R5, 6, 0:T], w_route[:, l, k, :], hT[:, k, :], start=(k == 0), stop=(k == KT - 1))
                mm.then_inc(S["logits"], 1)
                pe.wait_ge(S["biased"], l + 1)
                for c, (at, n) in enumerate(tok):
                    mm = pe.transpose(PS[0:n, 5, c * R5:(c + 1) * R5], logitsT[:, at:at + n], ident[0:R5, 0:R5])
                mm.then_inc(S["logits_up"], 1)
                rows(hT, "hrows", "hrows_sb", 2 * NT * l)
                pe.wait_ge(S["picked"], l + 1)
                for c, (at, n) in enumerate(tok):
                    for b in range(c + 1):
                        m = tok[b][1]
                        pe.matmul(PS[0:n, 7, c * NE:(c + 1) * NE], before[0:m, 0:n] if b == c else ones[0:m, 0:n],
                                  chosen_any[0:m, b, :], start=(b == 0), stop=(b == c))
                for c, (at, n) in enumerate(tok):
                    mm = pe.matmul(PS[:, 7, NT * NE:(NT + 1) * NE], ones[0:n, :], chosen_any[0:n, c, :],
                                   start=(c == 0), stop=(c == CH))
                mm.then_inc(S["counted"], 1)

            def rows(src, s, taken, base):
                for i in range(2 * NT):
                    at, n = tok[i // 2]
                    if i >= 4:
                        pe.wait_ge(S[taken], base + i - 3)
                    for j in range(4):
                        mm = pe.transpose(PS[0:n, i % 4, j * P:(j + 1) * P], src[:, (i % 2) * 4 + j, at:at + n], ident)
                    mm.then_inc(S[s], 1)

            def experts(l):
                el = E[l]

                def table_of(ready):
                    pe.wait_ge(el["hot"], ready)
                    for u in range(2):
                        for c, (_, m) in enumerate(tok):
                            for k in range(2):
                                mm = pe.matmul(PS[:, 7, 8 * u:8 * u + 6], hot[0:m, c, k, u * P:(u + 1) * P], marks[0:m, c, k, :],
                                               start=(c == 0 and k == 0), stop=(c == CH and k == 1))
                    mm.then_inc(el["tab"], 1)

                def rows_up(u, gathered, q):
                    pe.wait_ge(el[f"in{u}"], gathered)
                    pe.wait_ge(el["xt_sb"], q + 1)
                    for j in range(4):
                        mm = pe.transpose(PS[:, u, j * P:(j + 1) * P], x_slots[:, u, j * P:(j + 1) * P], ident)
                    mm.then_inc(el["xt"], 1)

                table_of(1)
                rows_up(0, 16, 0)
                pe.wait_ge(el["planned"], 1)
                pairs_n = pe.value_load(pairs[0:1, 0:1], min_val=NE // 2, max_val=NE // 2 + 5)

                def pair(i, w_in, w_down, weights):
                    for u in range(2):
                        q = 2 * i + u
                        weights(u, False)
                        pe.wait_ge(el["xt_sb"], AHEAD["xt_sb"] + q + 1)
                        pe.wait_ge(el["hid"], q + 1)
                        for k in range(KT):
                            for f in range(2):
                                mm = pe.matmul(PS[f * SLOT:(f + 1) * SLOT, 2 + u, 0:EF], x_slotsT[:, u, k % 4, k // 4, :],
                                               w_in[u][:, k, f, :], start=(k == 0), stop=(k == KT - 1))
                        mm.then_inc(el["gu"], 1)
                        if u == 0:
                            pe.wait_ge(el["idx"], i + 1)
                            table_of(i + 2)
                        rows_up(1 - u, 16 * (i + 1 + u), q + 1)
                        pe.wait_ge(el["hid"], AHEAD["hid"] + q + 1)
                        pe.wait_ge(el["ht_sb"], AHEAD["ht_sb"] + q)
                        pe.sem_inc(S["held"], 1)
                        for f in range(FB):
                            mm = pe.transpose(PS[:, 4, f * SLOT:(f + 1) * SLOT], hid[:, f * P:(f + 1) * P], ident[0:SLOT, 0:SLOT])
                        mm.then_inc(el["ht"], 1)
                        weights(u, True)
                        pe.wait_ge(el["ht_sb"], AHEAD["ht_sb"] + q + 1)
                        pe.wait_ge(el["y_sb"], q + 1)
                        for f in range(FB):
                            for half in range(2):
                                mm = pe.matmul(PS[half * SLOT:(half + 1) * SLOT, 5 + u, :], hidT[:, f, :],
                                               w_down[u][:, f, half * HALF:(half + 1) * HALF], start=(f == 0), stop=(f == FB - 1))
                        mm.then_inc(el["dn"], 1)

                def streamed(loads):
                    return lambda u, down: pe.wait_ge(el[f"wd{u}"], 16 * loads) if down else pe.wait_ge(el[f"w{u}"], 32 * loads)

                pair(0, ew_in, ew_down, streamed(1))
                pair(1, pre_in, pre_down, lambda u, down: None if down else pe.wait_ge(s_pre[u], 48 * (l + 1)))
                with pe.Fori(2, pairs_n) as i:
                    pair(i, ew_in, ew_down, streamed(i))

            pe.wait_ge(S["const_in"], 16)
            pe.wait_ge(S["x_in"], 32)
            for k in range(KT):
                if k >= 4:
                    pe.wait_ge(S["xt_sb"], k - 3)
                for c, (at, n) in enumerate(tok):
                    mm = pe.transpose(PS[:, k % 4, at:at + n], tokbuf[0:n, c, k * P:(k + 1) * P], ident[0:n, 0:n])
                mm.then_inc(S["xt"], 1)
                if k == 0:
                    pe.wait_ge(S["gains_in"], 16 * 6)
                    pe.transpose(PS[:, 6, 0:5 * KT + 2], gain_rows[:, :], ident[0:5 * KT + 2, 0:5 * KT + 2]).then_inc(S["prep"], 1)
            for j in range(4):
                mm = pe.transpose(PS[:, 5, j * P:(j + 1) * P], ws_in[:, j, :], ident)
            mm.then_inc(S["prep"], 1)
            pe.wait_ge(S["fill"], 5)
            mean_squares(0)
            pe.wait_ge(S["prep_sb"], 2)
            pe.matmul(PS[0:TSA, 6, 0:4 * TS], spread, wsT[0:TS, :, 0:TS], start=True, stop=True).then_inc(S["prep"], 1)
            for j in range(2 * KT):
                if j % (KT // 2) == 0 and j < KT:
                    pe.wait_ge(s_wv[j // (KT // 2)], 16)
                if j == KT:
                    pe.wait_ge(S["w_u_in"], 16)
                pe.wait_ge(S["z_sb"], j - 3) if j >= 4 else pe.wait_ge(S["xt_sb"], KT)
                tiles(j % 4, w_a if j < KT else w_b, (j % KT) * P, hT, S["z"],
                      (lambda k: (S["normed"], k + 1)) if j == 0 else None)
                if j == KT + 1:
                    mean_squares(1)
            pe.wait_ge(S["normed"], 2 * KT)
            pe.wait_ge(S["prep_sb"], 3)
            for i in range(2 * NT):
                at, n = tok[i // 2]
                if i >= 2:
                    pe.wait_ge(S["vtok_sb"], i - 1)
                for j in range(4):
                    mm = pe.transpose(PS[0:n, 4 + i % 2, j * P:(j + 1) * P], vT[:, (i % 2) * 4 + j, at:at + n], ident)
                mm.then_inc(S["vtok"], 1)
            pe.wait_ge(S["small_in"], 16 * (CH + NB + 4 * DEPTH))
            pe.wait_ge(S["z_sb"], 2 * KT)
            pe.wait_ge(S["vtok_sb"], 2 * NT)
            for j in range(KT):
                q = j // (KT // 4)
                if j >= 4:
                    pe.wait_ge(S["gated"], j - 3)
                pe.matmul(PS[:, j % 4, 0:T], ones[0:1, :], bs_row[:, q, :], start=True, stop=True)
                for c, (at, n) in enumerate(tok):
                    w = wsT[:, q, :] if c < CH else wsS[:, q, :]
                    mm = pe.matmul(PS[:, j % 4, at:at + n], tokbuf[0:n, c, j * P:(j + 1) * P], w,
                                   start=False, stop=True, skip_group_check=True)
                mm.then_inc(S["mixed"], 1)
            pe.wait_ge(S["w_out_in"], 16)
            project(0, uT, 2, lambda k: (S["gated"], k + 1))
            route(0)
            experts(0)
            for c, (at, n) in enumerate(tok):
                pe.wait_ge(S["yt"], c + 1)
                for k in Y_ORDER:
                    mm = pe.transpose(PS[:, k, at:at + n], tokbuf[0:n, c, k * P:(k + 1) * P], ident[0:n, 0:n])
                    if c == CH:
                        mm.then_inc(S["hrows_t"], 1)
            mean_squares(3)
            pe.wait_ge(S["w_q_in"], 16)
            for i in range(2 * KT):
                if i == KT:
                    pe.wait_ge(S["w_kv_in"], 16)
                if i >= 4:
                    pe.wait_ge(S["qkv_sb"], i - 3)
                tiles(i % 4, w_b if i < KT else w_a, (i % KT) * P, hT, S["qkv"],
                      (lambda k: (S["normed"], 3 * KT + k + 1)) if i == 0 else None)
                h = i - 1
                if 0 <= h < LH:
                    pe.wait_ge(S["hsq"], h + 1)
                    if h >= 2:
                        pe.wait_ge(S["hroot"], h - 1)
                    pe.matmul(PS[:, 4 + h % 2, 0:T], mean_h[:, :], sq[:, h % KT, :], start=True, stop=True).then_inc(S["hms"], 1)
                h = i - 3
                if 0 <= h < LH:
                    pe.wait_ge(S["hnormed"], h + 1)
                    if h >= 2:
                        pe.wait_ge(S["rsin"], h - 1)
                    pe.matmul(PS[0:ROT, 6 + h % 2, 0:T], rotate, zT[0:ROT, h, :], start=True, stop=True).then_inc(S["rot"], 1)
            pe.wait_ge(S["qkv_sb"], 2 * KT)
            pe.wait_ge(S["roped"], LH)
            for i in range(2 * NT):
                at, n = tok[i % NT]
                if i >= 4:
                    pe.wait_ge(S["kvt_sb"], i - 3)
                for a in range(KV):
                    mm = pe.transpose(PS[0:n, i % 4, a * P:(a + 1) * P], zT[:, NH + (i // NT) * KV + a, at:at + n], ident)
                mm.then_inc(S["kvt"], 1)
            pe.wait_ge(S["kvt_sb"], 2 * NT)
            for i in range(NU + 3):
                if i < NU:
                    h, c = units[i]
                    if i >= 2:
                        pe.wait_ge(S["pexp"], i - 1)
                    pe.matmul(PS[:, i % 2, 0:(c + 1) * P], zT[:, h, c * P:(c + 1) * P], zT[:, NH + h // G, 0:(c + 1) * P],
                              start=True, stop=True)
                    pe.matmul(PS[:, i % 2, c * P:(c + 1) * P], ident, causal_neg, start=False, stop=True,
                              skip_group_check=True).then_inc(S["ps"], 1)
                u = i - 2
                if 0 <= u < NU:
                    pe.wait_ge(S["pnorm"], u + 1)
                    if u >= 2:
                        pe.wait_ge(S["pt_sb"], u - 1)
                    for k in range(units[u][1] + 1):
                        mm = pe.transpose(PS[:, 2 + u % 2, k * P:(k + 1) * P], prob[:, u % 2, k * P:(k + 1) * P], ident)
                    mm.then_inc(S["pt"], 1)
                u = i - 3
                if 0 <= u:
                    h, c = units[u]
                    pe.wait_ge(S["pt_sb"], u + 1)
                    if u >= 2:
                        pe.wait_ge(S["po_sb"], u - 1)
                    for k in range(c + 1):
                        mm = pe.matmul(PS[:, 4 + u % 2, 0:P], vrow[:, k, (h // G) * P:(h // G + 1) * P],
                                       probT[:, u % 2, k * P:(k + 1) * P], start=(k == 0), stop=(k == c))
                    mm.then_inc(S["po"], 1)
            pe.wait_ge(S["po_sb"], NU)
            pe.wait_ge(S["gathered"], 2)
            with pe.Fori(0, NG) as g:
                def copied(n, more):
                    pe.wait_ge(S["kt_act" if n % 2 else "kt_dve"], 1 + g * (GRP * NPAGE // 2) + n // 2 + more)

                for half in range(2 * GRP + 1):
                    if half < 2 * GRP:
                        bb = half // 2
                        pe.wait_ge(s_k[bb % 2][half % 2], 16 * (NPAGE // 2) * (2 * g + bb // 2 + 1))
                        for n in range(4 * half, 4 * half + 4):
                            copied(n, 0)
                            for a in range(KV):
                                mm = pe.transpose(PS[:, n % 2, a * P:(a + 1) * P],
                                                  k_pages[:, bb % 2, n % NPAGE, a * P:(a + 1) * P], ident)
                            mm.then_inc(S["kt"], 1)
                    if half >= 1:
                        bb, part = divmod(half - 1, 2)
                        if half == 1:
                            pe.wait_ge(S["q_set"], (g + 1) * 2 * GRP)
                        copied(4 * half - 2, 1)
                        copied(4 * half - 1, 1)
                        for a in range(KV):
                            mm = pe.matmul(PS[a * HR:(a + 1) * HR, 6 + part, :], q_pad[:, bb, a, :], kts[(half - 1) % 2][:, a, :],
                                           start=(bb == 0), stop=(bb == GRP - 1))
                        mm.then_inc(S["sc"], 1)
                for a in range(KV):
                    mm = pe.matmul(PS[a * HR:(a + 1) * HR, 4, 0:TSA], q_all[:, a, :, :].rearrange("p b r -> p (b r)"),
                                   zT[:, NH + a, TP:T], start=True, stop=True)
                mm.then_inc(S["sn"], 1)
                pe.wait_ge(S["dnorm"], 2 * (g + 1))
                for j in range(NPAGE):
                    pe.transpose(PS[:, j // 4, (j % 4) * P:(j % 4 + 1) * P], Pd[:, j * P:(j + 1) * P], ident)
                pe.transpose(PS[0:TSA, 4, 0:P], Pn[:, :], ident).then_inc(S["dpt"], 1)
                pe.wait_ge(S["dpt_act"], g + 1)
                pe.wait_ge(S["dpt_dve"], 2 * (g + 1))
                for a in range(KV):
                    mm = pe.matmul(PS[:, 3, a * HR:(a + 1) * HR], vrow[0:TSA, CH, a * P:(a + 1) * P], PnT[:, a * HR:(a + 1) * HR],
                                   start=True, stop=True)
                mm.then_inc(S["new_v"], 1)
                for bb in range(GRP):
                    pe.wait_ge(s_v[bb], 16 * NPAGE * (g + 1))
                    for j in range(NPAGE):
                        for a in range(KV):
                            mm = pe.matmul(PS[a * HR:(a + 1) * HR, 5, bb * P:(bb + 1) * P], PdT[:, j, a * HR:(a + 1) * HR],
                                           v_pages[bb][:, j, a * P:(a + 1) * P], start=(j == 0), stop=(j == NPAGE - 1))
                    mm.then_inc(S["pv"], 1)
                pe.wait_ge(S["o_sb"], g + 1)
                for bb in range(GRP):
                    mm = pe.transpose(PS[:, 2, bb * P:(bb + 1) * P], o_rows[:, bb * P:(bb + 1) * P], ident)
                mm.then_inc(S["ot"], 1)
            pe.wait_ge(S["pv_sb"], NG * GRP)
            pe.wait_ge(S["w_o_in"], 16)
            project(KT, hT, 4)
            route(1)
            pe.wait_ge(S["hrows_sb"], 4 * NT)
            rows(xT, "xrows", "xrows_sb", 0)
            pe.wait_ge(S["xrows_sb"], 2 * NT)
            experts(1)


INPUTS = ["x_prompt", "x_sample", "cache_k", "cache_v", "page_table", "norm1", "norm2", "a_w_in", "a_g_v", "a_w_s",
          "a_b_s", "a_w_out", "b_w_qkv", "b_q_norm", "b_k_norm", "b_w_o", "moe_w_group", "moe_b_group",
          "moe_w_router", "moe_b_router", "moe_w_gate", "moe_w_up", "moe_w_down"]


def constants(TP, NB, TS, past):
    import numpy as np

    TSA = NB * TS
    T = TP + TSA
    cols, n = const_columns(T, TSA, TS)
    c = np.zeros((P, n), np.float32)
    row, col = np.arange(P)[:, None], np.arange(P)[None, :]
    c[:, cols["ident"]] = row == col
    c[:, cols["keep_upper"]] = row <= col
    c[:, cols["causal_neg"]] = np.where(col <= row, 0.0, NEG)
    half = ROT // 2
    pos = np.concatenate([np.arange(TP), np.tile(past + np.arange(TS), NB)]).astype(np.float32)
    inv = np.power(np.float32(THETA), -np.arange(half, dtype=np.float32) * np.float32(2.0) / np.float32(ROT))
    ang = inv[:, None].astype(np.float32) * pos[None, :]
    c[0:ROT, cols["cos"]] = np.tile(np.cos(ang), (2, 1))
    c[0:ROT, cols["sin"]] = np.tile(np.sin(ang), (2, 1))
    rotate = np.zeros((ROT, ROT), np.float32)
    for i in range(half):
        rotate[i + half, i] = -1.0
        rotate[i, i + half] = 1.0
    c[0:ROT, cols["rotate"]] = rotate
    r, q = np.arange(TSA)[:, None], np.arange(TSA)[None, :]
    c[0:TSA, cols["own_causal"]] = (r // TS == q // TS) & (r <= q)
    masks = []
    for g in range(NB // GRP):
        b, s = GRP * g + row // (G * TS) % GRP, row % TS
        masks.append(np.where((q // TS == b) & (q % TS <= s), 0.0, NEG))
    c[:, cols["own_neg"]] = np.concatenate(masks, 1)
    j, i = np.arange(16) // 4, np.arange(16) % 4
    c[:, cols["earlier"]] = i < j
    c[:, cols["later"]] = i > j
    c[0:TS, cols["spread"]] = np.arange(TS)[:, None] == q % TS
    c[:, cols["before"]] = row < col
    c[:, cols["limits"]] = SLOT * np.arange(1, 5)
    e = np.arange(16)
    c[:, cols["expert_tri"]] = (e[None, :] < e[:, None]).reshape(1, -1)
    c[:, cols["expert_slot"]] = SLOT * e
    c[:, cols["extra_slot"]] = SLOT * (15 - e)
    c[:, cols["extra_items"]] = np.arange(10)
    c[:, cols["evens"]] = 2 * np.arange(5)
    c[:, cols["first_items"]] = e
    c[:, cols["lanes"]] = np.tile(np.arange(SLOT), 4) + SLOT * (np.arange(2 * P) // P)
    nt = TP // P + 1
    half = (row[:, 0] >= SLOT).astype(np.float32)
    c[:, cols["halves"]] = np.stack([2 * P * nt + half, 4 * P * nt + half], 1)
    marks = np.zeros((P, nt, 2, 3), np.float32)
    marks[..., 0] = nt - np.arange(nt)[None, :, None]
    marks[..., 1] = row[:, :, None]
    marks[..., 2] = np.arange(2)[None, None, :]
    c[:, cols["marks"]] = marks.reshape(P, -1)
    return c


def kernel(**inputs):
    import numpy as np
    import concourse.bacc as bacc
    from concourse.bass_utils import run_bass_kernel_spmd

    nc = bacc.Bacc("TRN2", target_bir_lowering=False, num_devices=1)
    arrays, t = {}, {}
    for name in INPUTS:
        arrays[f"in_{name}"] = np.ascontiguousarray(inputs[name])
    _, TP, D = inputs["x_prompt"].shape
    NB, TS, _ = inputs["x_sample"].shape
    past = inputs["page_table"].shape[1] * inputs["cache_k"].shape[2]
    arrays["in_consts"] = constants(TP, NB, TS, past)
    for name in INPUTS + ["consts"]:
        a = arrays[f"in_{name}"]
        t[name] = nc.dram_tensor(f"in_{name}", a.shape, mybir.dt.from_np(a.dtype), kind="ExternalInput").ap()
    shapes = {"yp": (1, TP, D), "ys": (NB, TS, D), "kp": (1, 1, TP, KV, P), "vp": (1, 1, TP, KV, P),
              "ks": (1, NB, TS, KV, P), "vs": (1, NB, TS, KV, P), "chunk": (1, NB, TS, D)}
    o = {name: nc.dram_tensor(f"out_{name}", s, F32, kind="ExternalOutput").ap() for name, s in shapes.items()}
    hybrid_step(nc, t, o)
    r = run_bass_kernel_spmd(nc, [arrays], core_ids=[0])
    return tuple(r.results[0][f"out_{name}"] for name in shapes)
```
